# Optimizing a Trainium2 kernel written in Bass

```python
import math
import jax, jax.numpy as jnp
from jax import lax
import numpy as np

D_MODEL = 1024
BATCH = 1
SEQ = 256
DEPTH = 2

N_MIXERS = 4
EPS = 1e-6
Q_BLOCK = 128
CHUNK = 128

MLA_HEADS = 8
MLA_NOPE = 128
MLA_ROPE = 64
MLA_V = 128
MLA_Q_LORA = 384
MLA_KV_LORA = 256
ROPE_THETA = 10000.0

DIFF_HEADS = 8
DIFF_HD = D_MODEL // (2 * DIFF_HEADS)

MLSTM_HEADS = 8
MLSTM_QK = D_MODEL // 2 // MLSTM_HEADS
MLSTM_V = D_MODEL // MLSTM_HEADS

RET_HEADS = D_MODEL // 256
RET_QK = 256
RET_V = 2 * D_MODEL // RET_HEADS

FFN_HIDDEN = 2816
CONV_W = 3


def n_of(kind):
    return len(range(kind, DEPTH, N_MIXERS))

def rms_norm(x, g):
    xf = x.astype(jnp.float32)
    y = xf * lax.rsqrt(jnp.mean(xf * xf, -1, keepdims=True) + EPS)
    return (y * g.astype(jnp.float32)).astype(x.dtype)

def head_group_norm(x, g):
    xf = x.astype(jnp.float32)
    mu = jnp.mean(xf, -1, keepdims=True)
    xc = xf - mu
    y = xc * lax.rsqrt(jnp.mean(xc * xc, -1, keepdims=True) + EPS)
    return (y * g.astype(jnp.float32)).astype(x.dtype)

def query_blocks(t):
    b, s = t.shape[:2]
    return jnp.moveaxis(t.reshape(b, s // Q_BLOCK, Q_BLOCK, *t.shape[2:]), 1, 0)

def merge_blocks(t):
    t = jnp.moveaxis(t, 0, 1)
    return t.reshape(t.shape[0], -1, *t.shape[3:])

def rope_cos_sin(s, dim):
    inv = ROPE_THETA ** (-jnp.arange(0, dim, 2, dtype=jnp.float32) / dim)
    ang = jnp.arange(s, dtype=jnp.float32)[:, None] * inv[None, :]
    return jnp.cos(ang), jnp.sin(ang)

def apply_rope(x, cos, sin):
    half = x.shape[-1] // 2
    x1, x2 = x[..., :half], x[..., half:]
    cos = cos.astype(x.dtype)
    sin = sin.astype(x.dtype)
    return jnp.concatenate([x1 * cos - x2 * sin, x1 * sin + x2 * cos], -1)

def to_chunks(t):
    b, s = t.shape[:2]
    t = t.reshape(b, s // CHUNK, CHUNK, *t.shape[2:])
    return jnp.moveaxis(jnp.moveaxis(t, 1, 0), 3, 2)

def from_chunks(t):
    t = jnp.moveaxis(jnp.moveaxis(t, 2, 3), 0, 1)
    return t.reshape(t.shape[0], -1, *t.shape[3:])

def mla_mixer(x, w_dq, q_norm_g, w_uq, w_dkv, kv_norm_g, w_ukv, w_o):
    b, s, _ = x.shape
    H = MLA_HEADS
    cq = rms_norm(x @ w_dq, q_norm_g)
    q = (cq @ w_uq).reshape(b, s, H, MLA_NOPE + MLA_ROPE)
    ckv_kr = x @ w_dkv
    ckv = rms_norm(ckv_kr[..., :MLA_KV_LORA], kv_norm_g)
    kv = (ckv @ w_ukv).reshape(b, s, H, MLA_NOPE + MLA_V)
    k_nope, v = kv[..., :MLA_NOPE], kv[..., MLA_NOPE:]
    cos, sin = rope_cos_sin(s, MLA_ROPE)
    q_nope = q[..., :MLA_NOPE]
    q_rope = apply_rope(q[..., MLA_NOPE:], cos[:, None, :], sin[:, None, :])
    k_rope = apply_rope(ckv_kr[..., MLA_KV_LORA:], cos, sin)
    scale = (MLA_NOPE + MLA_ROPE) ** -0.5

    def block(args):
        qn, qr = args
        sc = (jnp.einsum('bqhd,bkhd->bhqk', qn, k_nope).astype(jnp.float32)
              + jnp.einsum('bqhr,bkr->bhqk', qr, k_rope).astype(jnp.float32)) * scale
        p = jax.nn.softmax(sc, -1).astype(v.dtype)
        return jnp.einsum('bhqk,bkhd->bqhd', p, v)

    o = merge_blocks(lax.map(block, (query_blocks(q_nope), query_blocks(q_rope))))
    return o.reshape(b, s, H * MLA_V) @ w_o

def diff_mixer(x, w_qkv, lam_p, subln_g, w_o, layer_idx):
    b, s, _ = x.shape
    H, d = DIFF_HEADS, DIFF_HD
    qkv = x @ w_qkv
    q = qkv[..., :2 * H * d].reshape(b, s, H, 2, d)
    k = qkv[..., 2 * H * d:4 * H * d].reshape(b, s, H, 2, d)
    v = qkv[..., 4 * H * d:].reshape(b, s, H, 2 * d)
    lam_init = 0.8 - 0.6 * math.exp(-0.3 * layer_idx)
    lp = lam_p.astype(jnp.float32)
    lam = jnp.exp(jnp.sum(lp[0] * lp[1])) - jnp.exp(jnp.sum(lp[2] * lp[3])) + lam_init
    slopes = 2.0 ** (-8.0 * jnp.arange(1, H + 1, dtype=jnp.float32) / H)
    pos = jnp.arange(s, dtype=jnp.int32)
    scale = d ** -0.5

    def block(args):
        qb, qpos = args
        sc = jnp.einsum('bqhjd,bkhjd->bhjqk', qb, k).astype(jnp.float32) * scale
        dist = jnp.abs(qpos[:, None] - pos[None, :]).astype(jnp.float32)
        sc = sc - slopes[None, :, None, None, None] * dist[None, None, None]
        p = jax.nn.softmax(sc, -1)
        a = (p[:, :, 0] - lam * p[:, :, 1]).astype(v.dtype)
        return jnp.einsum('bhqk,bkhd->bqhd', a, v)

    o = merge_blocks(lax.map(block, (query_blocks(q), pos.reshape(-1, Q_BLOCK))))
    o = rms_norm(o, subln_g) * (1.0 - lam_init)
    return o.reshape(b, s, H * 2 * d) @ w_o

def mlstm_chunkwise(q, k, v, i_pre, log_f):
    b, s, H, dk = q.shape
    dv = v.shape[-1]
    f32 = jnp.float32
    xs = (to_chunks(q.astype(f32)), to_chunks(k.astype(f32)), to_chunks(v.astype(f32)),
          to_chunks(i_pre), to_chunks(log_f))
    tri = jnp.tril(jnp.ones((CHUNK, CHUNK), bool))

    def step(carry, inp):
        C, n, m = carry
        qc, kc, vc, ic, fc = inp
        bcum = jnp.cumsum(fc, -1)
        dmat = jnp.where(tri, bcum[..., :, None] - bcum[..., None, :] + ic[..., None, :], -jnp.inf)
        m_inter = bcum + m[..., None]
        m_t = jnp.maximum(jnp.max(dmat, -1), m_inter)
        w_intra = jnp.exp(dmat - m_t[..., None])
        w_inter = jnp.exp(m_inter - m_t)
        sqk = jnp.einsum('bhtd,bhsd->bhts', qc, kc) * w_intra
        num = (w_inter[..., None] * jnp.einsum('bhtd,bhde->bhte', qc, C)
               + jnp.einsum('bhts,bhse->bhte', sqk, vc))
        den = w_inter * jnp.einsum('bhtd,bhd->bht', qc, n) + jnp.sum(sqk, -1)
        h = num / jnp.maximum(jnp.abs(den), jnp.exp(-m_t))[..., None]
        b_last = bcum[..., -1]
        g_s = b_last[..., None] - bcum + ic
        m_new = jnp.maximum(b_last + m, jnp.max(g_s, -1))
        w_s = jnp.exp(g_s - m_new[..., None])
        decay = jnp.exp(b_last + m - m_new)
        C_new = decay[..., None, None] * C + jnp.einsum('bhs,bhsd,bhse->bhde', w_s, kc, vc)
        n_new = decay[..., None] * n + jnp.einsum('bhs,bhsd->bhd', w_s, kc)
        return (C_new, n_new, m_new), h

    init = (jnp.zeros((b, H, dk, dv), f32), jnp.zeros((b, H, dk), f32), jnp.zeros((b, H), f32))
    _, hs = lax.scan(step, init, xs)
    return from_chunks(hs).astype(v.dtype)

def mlstm_mixer(x, w_in, b_gates, norm_g, w_out):
    b, s, _ = x.shape
    H, dk, dv = MLSTM_HEADS, MLSTM_QK, MLSTM_V
    proj = x @ w_in
    o1, o2, o3, o4 = H * dk, 2 * H * dk, 2 * H * dk + H * dv, 2 * H * dk + 2 * H * dv
    q = proj[..., :o1].reshape(b, s, H, dk)
    k = proj[..., o1:o2].reshape(b, s, H, dk) * (dk ** -0.5)
    v = proj[..., o2:o3].reshape(b, s, H, dv)
    o_gate = jax.nn.sigmoid(proj[..., o3:o4])
    g = (proj[..., o4:] + b_gates).astype(jnp.float32).reshape(b, s, 4, H)
    h_f = mlstm_chunkwise(q, k, v, g[:, :, 0], jax.nn.log_sigmoid(g[:, :, 1]))
    fl = lambda t: jnp.flip(t, 1)
    h_b = fl(mlstm_chunkwise(fl(q), fl(k), fl(v), fl(g[:, :, 2]), jax.nn.log_sigmoid(fl(g[:, :, 3]))))
    h = head_group_norm(h_f + h_b, norm_g.reshape(H, dv))
    return (h.reshape(b, s, H * dv) * o_gate) @ w_out

def retention_chunkwise(q, k, v, log_gamma):
    b, s, H, dk = q.shape
    dv = v.shape[-1]
    f32 = jnp.float32
    idx = jnp.arange(CHUNK, dtype=f32)
    rel = idx[:, None] - idx[None, :]
    dmask = jnp.exp(jnp.maximum(rel, 0.0)[None] * log_gamma[:, None, None]) * (rel >= 0)[None]
    xi = jnp.exp((idx[None] + 1.0) * log_gamma[:, None])
    zeta = jnp.exp((CHUNK - 1.0 - idx[None]) * log_gamma[:, None])
    g_chunk = jnp.exp(CHUNK * log_gamma)
    xs = (to_chunks(q.astype(f32)), to_chunks(k.astype(f32)), to_chunks(v.astype(f32)))

    def step(R, inp):
        qc, kc, vc = inp
        inner = jnp.einsum('bhts,bhse->bhte', jnp.einsum('bhtd,bhsd->bhts', qc, kc) * dmask, vc)
        cross = jnp.einsum('bhtd,bhde->bhte', qc, R) * xi[None, :, :, None]
        R_new = g_chunk[None, :, None, None] * R + jnp.einsum('bhsd,bhse->bhde', kc * zeta[None, :, :, None], vc)
        return R_new, inner + cross

    _, ys = lax.scan(step, jnp.zeros((b, H, dk, dv), f32), xs)
    return from_chunks(ys).astype(v.dtype)

def retention_mixer(x, w_in, decay_logit, norm_g, w_o):
    b, s, _ = x.shape
    H, dk, dv = RET_HEADS, RET_QK, RET_V
    proj = x @ w_in
    o1, o2, o3 = H * dk, 2 * H * dk, 2 * H * dk + H * dv
    q = proj[..., :o1].reshape(b, s, H, dk)
    k = proj[..., o1:o2].reshape(b, s, H, dk) * (dk ** -0.5)
    v = proj[..., o2:o3].reshape(b, s, H, dv)
    gate = proj[..., o3:]
    lg = jax.nn.log_sigmoid(decay_logit.astype(jnp.float32))
    fl = lambda t: jnp.flip(t, 1)
    y = retention_chunkwise(q, k, v, lg[0]) + fl(retention_chunkwise(fl(q), fl(k), fl(v), lg[1]))
    y = head_group_norm(y, norm_g.reshape(H, dv)).reshape(b, s, H * dv)
    return (jax.nn.silu(gate) * y) @ w_o

def conv_ffn(x, w_up, conv_w, conv_b, w_down):
    u = x @ w_up
    s = u.shape[1]
    half = CONV_W // 2
    up = jnp.pad(u, ((0, 0), (half, half), (0, 0)))
    c = conv_b
    for j in range(CONV_W):
        c = c + conv_w[j] * up[:, j:j + s]
    g, val = c[..., :FFN_HIDDEN], c[..., FFN_HIDDEN:]
    return (jax.nn.gelu(g) * val) @ w_down

def first_inputs(seed: int = 0) -> dict:
    key = jax.random.key(seed)
    ks = iter(jax.random.split(key, 40))
    D = D_MODEL
    nA, nB, nC, nD = n_of(0), n_of(1), n_of(2), n_of(3)

    def w(shape, fan_in):
        return jax.random.normal(next(ks), shape, jnp.float32) * (fan_in ** -0.5)

    def gain(shape):
        return 1.0 + 0.02 * jax.random.normal(next(ks), shape, jnp.float32)

    inp = {}
    inp['x'] = jax.random.normal(next(ks), (BATCH, SEQ, D), jnp.float32)
    inp['norm_g'] = gain((DEPTH, 4, D))
    inp['ffn_w_up'] = w((DEPTH, D, 2 * FFN_HIDDEN), D)
    inp['ffn_conv_w'] = w((DEPTH, CONV_W, 2 * FFN_HIDDEN), CONV_W)
    inp['ffn_conv_b'] = 0.01 * jax.random.normal(next(ks), (DEPTH, 2 * FFN_HIDDEN), jnp.float32)
    inp['ffn_w_down'] = w((DEPTH, FFN_HIDDEN, D), FFN_HIDDEN)
    inp['mla_w_dq'] = w((nA, D, MLA_Q_LORA), D)
    inp['mla_q_norm_g'] = gain((nA, MLA_Q_LORA))
    inp['mla_w_uq'] = w((nA, MLA_Q_LORA, MLA_HEADS * (MLA_NOPE + MLA_ROPE)), MLA_Q_LORA)
    inp['mla_w_dkv'] = w((nA, D, MLA_KV_LORA + MLA_ROPE), D)
    inp['mla_kv_norm_g'] = gain((nA, MLA_KV_LORA))
    inp['mla_w_ukv'] = w((nA, MLA_KV_LORA, MLA_HEADS * (MLA_NOPE + MLA_V)), MLA_KV_LORA)
    inp['mla_w_o'] = w((nA, MLA_HEADS * MLA_V, D), MLA_HEADS * MLA_V)
    inp['diff_w_qkv'] = w((nB, D, 3 * D), D)
    inp['diff_lambda'] = 0.1 * jax.random.normal(next(ks), (nB, 4, DIFF_HD), jnp.float32)
    inp['diff_subln_g'] = gain((nB, 2 * DIFF_HD))
    inp['diff_w_o'] = w((nB, D, D), D)
    H = MLSTM_HEADS
    inp['mlstm_w_in'] = w((nC, D, 2 * H * MLSTM_QK + 2 * H * MLSTM_V + 4 * H), D)
    i_bias = 0.1 * jax.random.normal(next(ks), (nC, 2, H), jnp.float32)
    f_bias = jnp.linspace(3.0, 6.0, H, dtype=jnp.float32)[None, None] + 0.1 * jax.random.normal(next(ks), (nC, 2, H), jnp.float32)
    inp['mlstm_b_gates'] = jnp.stack([i_bias[:, 0], f_bias[:, 0], i_bias[:, 1], f_bias[:, 1]], 1).reshape(nC, 4 * H)
    inp['mlstm_norm_g'] = gain((nC, H * MLSTM_V))
    inp['mlstm_w_out'] = w((nC, H * MLSTM_V, D), H * MLSTM_V)
    Hr = RET_HEADS
    inp['ret_w_in'] = w((nD, D, 2 * Hr * RET_QK + 2 * Hr * RET_V), D)
    eps_h = 2.0 ** (-5.0 - np.arange(Hr, dtype=np.float32))
    base_logit = jnp.asarray(np.log((1.0 - eps_h) / eps_h), jnp.float32)
    inp['ret_decay_logit'] = base_logit[None, None] + 0.1 * jax.random.normal(next(ks), (nD, 2, Hr), jnp.float32)
    inp['ret_norm_g'] = gain((nD, Hr * RET_V))
    inp['ret_w_o'] = w((nD, Hr * RET_V, D), Hr * RET_V)
    return inp

def first_block(x, norm_g, ffn_w_up, ffn_conv_w, ffn_conv_b, ffn_w_down,
              mla_w_dq, mla_q_norm_g, mla_w_uq, mla_w_dkv, mla_kv_norm_g, mla_w_ukv, mla_w_o,
              diff_w_qkv, diff_lambda, diff_subln_g, diff_w_o,
              mlstm_w_in, mlstm_b_gates, mlstm_norm_g, mlstm_w_out,
              ret_w_in, ret_decay_logit, ret_norm_g, ret_w_o):
    h = x
    for i in range(DEPTH):
        kind, j = i % N_MIXERS, i // N_MIXERS
        a = rms_norm(h, norm_g[i, 0])
        if kind == 0:
            a = mla_mixer(a, mla_w_dq[j], mla_q_norm_g[j], mla_w_uq[j], mla_w_dkv[j],
                          mla_kv_norm_g[j], mla_w_ukv[j], mla_w_o[j])
        elif kind == 1:
            a = diff_mixer(a, diff_w_qkv[j], diff_lambda[j], diff_subln_g[j], diff_w_o[j], i)
        elif kind == 2:
            a = mlstm_mixer(a, mlstm_w_in[j], mlstm_b_gates[j], mlstm_norm_g[j], mlstm_w_out[j])
        else:
            a = retention_mixer(a, ret_w_in[j], ret_decay_logit[j], ret_norm_g[j], ret_w_o[j])
        h = h + rms_norm(a, norm_g[i, 1])
        f = conv_ffn(rms_norm(h, norm_g[i, 2]), ffn_w_up[i], ffn_conv_w[i], ffn_conv_b[i], ffn_w_down[i])
        h = h + rms_norm(f, norm_g[i, 3])
    return h


DEPTH_2 = 1

HEAD_DIM = 64
MOBA_HEADS = 8
MOBA_BLOCK = 256
MOBA_TOPK = 3
DSA_HEADS = 8
DSA_MAX_TOPK = 256
IDX_HEADS = 8
IDX_DIM = 64
N_GROUPS = 4
EXPERTS_PER_GROUP = 8
N_EXPERTS = N_GROUPS * EXPERTS_PER_GROUP
EXPERT_TOPK = 2
EXPERT_FF = 512
DISPATCH_BLOCK = 256
Q_CHUNK = 128
RMS_EPS = 1e-6
NEG = -1e30

MOBA_WIDTH = MOBA_HEADS * HEAD_DIM
DSA_WIDTH = DSA_HEADS * HEAD_DIM
IDX_SCALE = (IDX_HEADS * IDX_DIM) ** -0.5
IN_SIZES = (MOBA_WIDTH,) * 3 + (DSA_WIDTH,) * 3 + (IDX_HEADS * IDX_DIM, IDX_DIM, IDX_HEADS, D_MODEL, D_MODEL)
IN_COLS = sum(IN_SIZES)
SPLIT_POINTS = tuple(int(v) for v in np.cumsum(IN_SIZES)[:-1])


def rms_norm_2(x, g):
    xf = x.astype(jnp.float32)
    y = xf * lax.rsqrt(jnp.mean(xf * xf, axis=-1, keepdims=True) + RMS_EPS)
    return (y * g.astype(jnp.float32)).astype(x.dtype)

def rope(x):
    s, d = x.shape[1], x.shape[-1]
    inv = jnp.power(ROPE_THETA, -jnp.arange(0, d, 2, dtype=jnp.float32) / d)
    ang = jnp.arange(s, dtype=jnp.float32)[:, None] * inv[None, :]
    ang = ang.reshape((s,) + (1,) * (x.ndim - 3) + (d // 2,))
    cos, sin = jnp.cos(ang), jnp.sin(ang)
    x1, x2 = jnp.split(x.astype(jnp.float32), 2, axis=-1)
    return jnp.concatenate([x1 * cos - x2 * sin, x1 * sin + x2 * cos], axis=-1).astype(x.dtype)

def masked_softmax(scores, mask):
    return jax.nn.softmax(jnp.where(mask, scores.astype(jnp.float32), NEG), axis=-1)

def moba_attend(q, k, v):
    h, s, d = q.shape
    nb = -(-s // MOBA_BLOCK)
    pad = nb * MOBA_BLOCK - s
    kb = jnp.pad(k, ((0, 0), (0, pad), (0, 0))).reshape(h, nb, MOBA_BLOCK, d)
    vb = jnp.pad(v, ((0, 0), (0, pad), (0, 0))).reshape(h, nb, MOBA_BLOCK, d)
    n_sel = max(1, min(MOBA_TOPK, nb - 1))
    own = jnp.arange(s) // MOBA_BLOCK
    k_mean = jnp.mean(kb.astype(jnp.float32), axis=2)
    gate = jnp.einsum('hsd,hnd->hsn', q.astype(jnp.float32), k_mean)
    past = jnp.arange(nb)[None, :] < own[:, None]
    gate = jnp.where(past[None], gate, NEG)
    _, sel = lax.top_k(gate, n_sel)
    sel_ok = sel < own[None, :, None]
    n_chunks = s // Q_CHUNK
    qc = q.reshape(h, n_chunks, Q_CHUNK, d).transpose(1, 0, 2, 3)
    selc = sel.reshape(h, n_chunks, Q_CHUNK, n_sel).transpose(1, 0, 2, 3)
    okc = sel_ok.reshape(h, n_chunks, Q_CHUNK, n_sel).transpose(1, 0, 2, 3)
    scale = d ** -0.5
    head_ix = jnp.arange(h)[:, None, None]

    def one_chunk(args):
        qi, si, oki, c = args
        q_pos = c * Q_CHUNK + jnp.arange(Q_CHUNK)
        blk = (c * Q_CHUNK) // MOBA_BLOCK
        k_sel = kb[head_ix, si]
        v_sel = vb[head_ix, si]
        k_own = lax.dynamic_index_in_dim(kb, blk, axis=1, keepdims=False)
        v_own = lax.dynamic_index_in_dim(vb, blk, axis=1, keepdims=False)
        s_sel = jnp.einsum('hqd,hqnkd->hqnk', qi, k_sel).reshape(h, Q_CHUNK, n_sel * MOBA_BLOCK) * scale
        s_own = jnp.einsum('hqd,hkd->hqk', qi, k_own) * scale
        m_sel = jnp.broadcast_to(oki[..., None], oki.shape + (MOBA_BLOCK,)).reshape(h, Q_CHUNK, n_sel * MOBA_BLOCK)
        k_pos = blk * MOBA_BLOCK + jnp.arange(MOBA_BLOCK)
        m_own = jnp.broadcast_to((k_pos[None, :] <= q_pos[:, None])[None], (h, Q_CHUNK, MOBA_BLOCK))
        p = masked_softmax(jnp.concatenate([s_sel, s_own], axis=-1),
                           jnp.concatenate([m_sel, m_own], axis=-1)).astype(v.dtype)
        p_sel = p[..., :n_sel * MOBA_BLOCK].reshape(h, Q_CHUNK, n_sel, MOBA_BLOCK)
        p_own = p[..., n_sel * MOBA_BLOCK:]
        return (jnp.einsum('hqnk,hqnkd->hqd', p_sel, v_sel)
                + jnp.einsum('hqk,hkd->hqd', p_own, v_own))

    out = lax.map(one_chunk, (qc, selc, okc, jnp.arange(n_chunks)))
    return out.transpose(1, 0, 2, 3).reshape(h, s, d)

def dsa_attend(q, k, v, q_idx, k_idx, w_idx):
    h, s, d = q.shape
    top = min(DSA_MAX_TOPK, s // 4)
    n_chunks = s // Q_CHUNK
    qc = q.reshape(h, n_chunks, Q_CHUNK, d).transpose(1, 0, 2, 3)
    qic = q_idx.reshape(n_chunks, Q_CHUNK, IDX_HEADS, IDX_DIM)
    wic = w_idx.reshape(n_chunks, Q_CHUNK, IDX_HEADS)
    k_pos = jnp.arange(s)
    kf = k_idx.astype(jnp.float32)
    scale = d ** -0.5

    def one_chunk(args):
        qi, qii, wi, c = args
        q_pos = c * Q_CHUNK + jnp.arange(Q_CHUNK)
        logits = jnp.einsum('qhd,sd->qhs', qii.astype(jnp.float32), kf)
        score = jnp.einsum('qh,qhs->qs', wi.astype(jnp.float32), jax.nn.relu(logits))
        score = jnp.where(k_pos[None, :] <= q_pos[:, None], score, NEG)
        _, idx = lax.top_k(score, top)
        ok = idx <= q_pos[:, None]
        k_sel = k[:, idx]
        v_sel = v[:, idx]
        sc = jnp.einsum('hqd,hqkd->hqk', qi, k_sel) * scale
        p = masked_softmax(sc, ok[None]).astype(v.dtype)
        return jnp.einsum('hqk,hqkd->hqd', p, v_sel)

    out = lax.map(one_chunk, (qc, qic, wic, jnp.arange(n_chunks)))
    return out.transpose(1, 0, 2, 3).reshape(h, s, d)

def hier_moe(h, w_group, b_group, w_expert, b_expert, w1, w3, w2):
    b, s, d = h.shape
    t = b * s
    xt = h.reshape(t, d)
    g_logit = (xt @ w_group + b_group).astype(jnp.float32)
    g_prob = jax.nn.softmax(g_logit, axis=-1)
    g_sel = jnp.argmax(g_logit, axis=-1)
    g_w = jnp.take_along_axis(g_prob, g_sel[:, None], axis=1)
    e_logit = (xt @ w_expert + b_expert).astype(jnp.float32).reshape(t, N_GROUPS, EXPERTS_PER_GROUP)
    e_logit = jnp.take_along_axis(e_logit, g_sel[:, None, None], axis=1)[:, 0]
    top_p, top_i = lax.top_k(jax.nn.softmax(e_logit, axis=-1), EXPERT_TOPK)
    gate = g_w * top_p / jnp.sum(top_p, axis=-1, keepdims=True)
    expert = g_sel[:, None] * EXPERTS_PER_GROUP + top_i
    n_asg = t * EXPERT_TOPK
    e_flat = expert.reshape(-1)
    order = jnp.argsort(e_flat)
    e_sorted = e_flat[order]
    tok_sorted = order // EXPERT_TOPK
    gate_sorted = gate.reshape(-1)[order].astype(h.dtype)
    counts = jnp.bincount(e_flat, length=N_EXPERTS)
    padded = (counts + DISPATCH_BLOCK - 1) // DISPATCH_BLOCK * DISPATCH_BLOCK
    ends = jnp.cumsum(padded)
    starts_pad = ends - padded
    starts = jnp.cumsum(counts) - counts
    dest = starts_pad[e_sorted] + jnp.arange(n_asg) - starts[e_sorted]
    n_blocks = -(-n_asg // DISPATCH_BLOCK) + N_EXPERTS
    xs = jnp.zeros((n_blocks * DISPATCH_BLOCK, d), h.dtype).at[dest].set(xt[tok_sorted])
    block_expert = jnp.minimum(
        jnp.searchsorted(ends, jnp.arange(n_blocks) * DISPATCH_BLOCK, side='right'), N_EXPERTS - 1)

    def expert_block(args):
        xb, e = args
        hid = jax.nn.silu(xb @ w1[e]) * (xb @ w3[e])
        return hid @ w2[e]

    ys = lax.map(expert_block, (xs.reshape(n_blocks, DISPATCH_BLOCK, d), block_expert)).reshape(-1, d)
    out = jax.ops.segment_sum(ys[dest] * gate_sorted[:, None], tok_sorted, num_segments=t)
    return out.reshape(b, s, d)

def hybrid_layer(x, g_mix, w_in, w_proj_a, w_proj_b, w_out, g_ffn,
                 w_group, b_group, w_expert, b_expert, w1, w3, w2):
    b, s, _ = x.shape
    h = rms_norm_2(x, g_mix)
    qa, ka, va, qb, kb, vb, qi, ki, wi, ga, gb = jnp.split(h @ w_in, SPLIT_POINTS, axis=-1)

    def heads(t, n):
        return t.reshape(b, s, n, HEAD_DIM)

    qa = rope(heads(qa, MOBA_HEADS)).transpose(0, 2, 1, 3)
    ka = rope(heads(ka, MOBA_HEADS)).transpose(0, 2, 1, 3)
    va = heads(va, MOBA_HEADS).transpose(0, 2, 1, 3)
    qb = rope(heads(qb, DSA_HEADS)).transpose(0, 2, 1, 3)
    kb = rope(heads(kb, DSA_HEADS)).transpose(0, 2, 1, 3)
    vb = heads(vb, DSA_HEADS).transpose(0, 2, 1, 3)
    qi = rope(qi.reshape(b, s, IDX_HEADS, IDX_DIM))
    ki = rope(ki)
    wi = wi * IDX_SCALE
    o_a = lax.map(lambda a: moba_attend(*a), (qa, ka, va))
    o_b = lax.map(lambda a: dsa_attend(*a), (qb, kb, vb, qi, ki, wi))
    o_a = o_a.transpose(0, 2, 1, 3).reshape(b, s, MOBA_WIDTH)
    o_b = o_b.transpose(0, 2, 1, 3).reshape(b, s, DSA_WIDTH)
    mixed = jax.nn.sigmoid(ga) * (o_a @ w_proj_a) + jax.nn.sigmoid(gb) * (o_b @ w_proj_b)
    x = x + mixed @ w_out
    x = x + hier_moe(rms_norm_2(x, g_ffn), w_group, b_group, w_expert, b_expert, w1, w3, w2)
    return x

def second_inputs(seed: int = 0) -> dict:
    key = jax.random.key(seed)
    ks = jax.random.split(key, 16)
    nrm = jax.random.normal
    f32 = jnp.float32
    return {
        "x": nrm(ks[0], (BATCH, SEQ, D_MODEL), f32),
        "g_mix": 1.0 + 0.02 * nrm(ks[1], (DEPTH_2, D_MODEL), f32),
        "w_in": nrm(ks[2], (DEPTH_2, D_MODEL, IN_COLS), f32) * D_MODEL ** -0.5,
        "w_proj_a": nrm(ks[3], (DEPTH_2, MOBA_WIDTH, D_MODEL), f32) * MOBA_WIDTH ** -0.5,
        "w_proj_b": nrm(ks[4], (DEPTH_2, DSA_WIDTH, D_MODEL), f32) * DSA_WIDTH ** -0.5,
        "w_out": nrm(ks[5], (DEPTH_2, D_MODEL, D_MODEL), f32) * D_MODEL ** -0.5,
        "g_ffn": 1.0 + 0.02 * nrm(ks[6], (DEPTH_2, D_MODEL), f32),
        "w_group": nrm(ks[7], (DEPTH_2, D_MODEL, N_GROUPS), f32) * D_MODEL ** -0.5,
        "b_group": 0.01 * nrm(ks[8], (DEPTH_2, N_GROUPS), f32),
        "w_expert": nrm(ks[9], (DEPTH_2, D_MODEL, N_EXPERTS), f32) * D_MODEL ** -0.5,
        "b_expert": 0.01 * nrm(ks[10], (DEPTH_2, N_EXPERTS), f32),
        "w1": nrm(ks[11], (DEPTH_2, N_EXPERTS, D_MODEL, EXPERT_FF), f32) * D_MODEL ** -0.5,
        "w3": nrm(ks[12], (DEPTH_2, N_EXPERTS, D_MODEL, EXPERT_FF), f32) * D_MODEL ** -0.5,
        "w2": nrm(ks[13], (DEPTH_2, N_EXPERTS, EXPERT_FF, D_MODEL), f32) * EXPERT_FF ** -0.5,
        "g_final": 1.0 + 0.02 * nrm(ks[14], (D_MODEL,), f32),
    }

def second_block(x, g_mix, w_in, w_proj_a, w_proj_b, w_out, g_ffn,
              w_group, b_group, w_expert, b_expert, w1, w3, w2, g_final):
    for l in range(DEPTH_2):
        x = hybrid_layer(x, g_mix[l], w_in[l], w_proj_a[l], w_proj_b[l], w_out[l], g_ffn[l],
                         w_group[l], b_group[l], w_expert[l], b_expert[l], w1[l], w3[l], w2[l])
    return rms_norm_2(x, g_final)


def setup_inputs(seed=0):
    out = dict(first_inputs(seed))
    for name, value in second_inputs(seed + 1).items():
        if name != "x":
            out[name + "_2"] = value
    return out


def reference(
    x, norm_g, ffn_w_up, ffn_conv_w, ffn_conv_b, ffn_w_down, mla_w_dq, mla_q_norm_g, mla_w_uq,
    mla_w_dkv, mla_kv_norm_g, mla_w_ukv, mla_w_o, diff_w_qkv, diff_lambda, diff_subln_g,
    diff_w_o, mlstm_w_in, mlstm_b_gates, mlstm_norm_g, mlstm_w_out, ret_w_in, ret_decay_logit,
    ret_norm_g, ret_w_o, g_mix_2, w_in_2, w_proj_a_2, w_proj_b_2, w_out_2, g_ffn_2, w_group_2,
    b_group_2, w_expert_2, b_expert_2, w1_2, w3_2, w2_2, g_final_2,
):
    x = first_block(
        x, norm_g, ffn_w_up, ffn_conv_w, ffn_conv_b, ffn_w_down, mla_w_dq, mla_q_norm_g,
        mla_w_uq, mla_w_dkv, mla_kv_norm_g, mla_w_ukv, mla_w_o, diff_w_qkv, diff_lambda,
        diff_subln_g, diff_w_o, mlstm_w_in, mlstm_b_gates, mlstm_norm_g, mlstm_w_out, ret_w_in,
        ret_decay_logit, ret_norm_g, ret_w_o,
    )
    return second_block(
        x, g_mix_2, w_in_2, w_proj_a_2, w_proj_b_2, w_out_2, g_ffn_2, w_group_2, b_group_2,
        w_expert_2, b_expert_2, w1_2, w3_2, w2_2, g_final_2,
    )


_drawn_inputs = setup_inputs


def setup_inputs(seed=0):
    import zlib

    import numpy as np

    out = dict(_drawn_inputs(seed))
    spreads = {}
    factors = {'ffn_conv_b': 3.262,
     'diff_subln_g': 3.859,
     'g_mix_2': 4.96,
     'g_ffn_2': 4.033,
     'b_group_2': 8.0,
     'b_expert_2': 8.0,
     'g_final_2': 2.836}
    for name, (base, spread) in spreads.items():
        noise = np.random.default_rng([zlib.crc32(name.encode()), seed]).standard_normal(out[name].shape)
        drawn = base * np.exp(spread * noise) if base else spread * noise
        out[name] = __import__('jax').numpy.asarray(drawn.astype(out[name].dtype))
    for name, factor in factors.items():
        out[name] = (out[name] * factor).astype(out[name].dtype)
    return out
```

```python
from contextlib import ExitStack

import numpy as np

import concourse.bass as bass
from concourse import mybir

F32 = mybir.dt.float32
I32 = mybir.dt.int32
ALU = mybir.AluOpType
ACT = mybir.ActivationFunctionType
AX = mybir.AxisListType.X

P = 128
S = 256
NT = S // P
D = 1024
KT = D // P
EPS = 1e-6
NEG = -1e30

QL, KVL = 384, 256
MH, MN, MR = 8, 128, 64
MLA_SCALE = float(MN + MR) ** -0.5
DH = 8
HD = 64
HD_SCALE = float(HD) ** -0.5
F = 2816
FT = F // P
FM = FT // 2
LAM_INIT = 0.8 - 0.6 * float(np.exp(-0.3))
TOPK = min(256, S // 4)
IDX_SCALE = float(8 * 64) ** -0.5
NE, EF = 32, 512
NG, EPG = 4, 8
CAP = 64
ROUNDS = S // CAP
NP = NE // 2

RING = 6
SLOT = 4096

C_ID, C_TRI, C_ONE, C_ZERO, C_IOTA = 0, 128, 256, 384, 512
C_DIST = 576
C_CAUS = C_DIST + NT * S
C_COS = C_CAUS + NT * S
C_SIN = C_COS + NT * HD
C_END = C_SIN + NT * HD

G_N = [0, 8, 16, 24, 32, 40]
G_Q, G_KV, G_SUB = 48, 51, 53
G_END = 54


def constants():
    c = np.zeros((P, C_END), np.float32)
    i = np.arange(P)
    c[:, C_ID:C_ID + P] = np.eye(P)
    c[:, C_TRI:C_TRI + P] = i[:, None] < i[None, :]
    c[:, C_ONE:C_ONE + P] = 1.0
    c[:, C_IOTA:C_IOTA + CAP] = np.arange(CAP)[None]
    k = np.arange(S)
    inv = np.float32(10000.0) ** (-np.arange(0, HD, 2, dtype=np.float32) / np.float32(HD))
    for t in range(NT):
        q = i + t * P
        c[:, C_DIST + t * S:C_DIST + (t + 1) * S] = np.abs(q[:, None] - k[None, :])
        c[:, C_CAUS + t * S:C_CAUS + (t + 1) * S] = np.where(k[None, :] <= q[:, None], 0.0, NEG)
        ang = q.astype(np.float32)[:, None] * inv[None, :]
        c[:, C_COS + t * HD:C_COS + (t + 1) * HD] = np.tile(np.cos(ang), 2)
        c[:, C_SIN + t * HD:C_SIN + t * HD + 32] = -np.sin(ang)
        c[:, C_SIN + t * HD + 32:C_SIN + (t + 1) * HD] = np.sin(ang)
    return c


def attention_groups(base, heads, maps):
    sc, tr, ou, g = {}, {}, {}, base
    for s in range(heads + 2):
        if s < heads:
            for j in range(maps):
                sc[s, j] = g
                g += 1
        if 1 <= s <= heads:
            tr[s - 1] = g
            g += 1
        if s >= 2:
            ou[s - 2] = g
            g += 1
    return sc, tr, ou, g - base


def plan():
    G, g = {}, 0
    for name, n in [
        ("par", 3), ("x0", 4), ("mla_down", 4), ("mla_t", 2), ("mla_t2", 2), ("mla_qn", 4), ("mla_qr", 2),
        ("mla_kn", 4), ("mla_v", 4), ("mla_qrt", 2), ("mla_att", attention_groups(0, MH, 1)[3]), ("mla_o", 4),
        ("x1", 4), ("x2", 4),
        ("diff_q", 4), ("diff_k", 4), ("diff_v", 4), ("diff_att", attention_groups(0, DH, 2)[3]),
        ("diff_t", 4), ("diff_o", 4), ("x3", 4), ("x4", 4),
        ("qi", 2), ("qi_t", 2), ("ki", 2), ("ki_t", 2), ("index", 8),
        ("qa", 2), ("qa_t", 2), ("ka", 2), ("ka_t", 2), ("va", 2),
        ("qb", 2), ("qb_t", 2), ("kb", 2), ("kb_t", 2), ("vb", 2),
        ("moba_att", attention_groups(0, 8, 1)[3]), ("dsa_att", attention_groups(0, 8, 1)[3]),
        ("gates", 8), ("pa", 4), ("pb", 4), ("mix_t", 4), ("hyb_o", 4), ("x5", 4), ("router", 2), ("pos", 1),
    ]:
        G[name] = g
        g += n
    C, c = {}, 0
    for name, n in [
        ("dq", 1), ("dkv", 1), ("uq", 2), ("ukv", 1), ("mla_wo", 2), ("ffn0", 2 * FM),
        ("qkv", 6), ("diff_wo", 2), ("ffn1", 2 * FM),
        ("qi", 1), ("ki", 1), ("qa", 1), ("ka", 1), ("va", 1), ("qb", 1), ("kb", 1), ("vb", 1),
        ("gates", 4), ("pa", 1), ("pb", 1), ("wout", 2), ("moe", 6 * NP),
    ]:
        C[name] = c
        c += n
    return G, C


def build(nc, A, cst, out):
    G, C = plan()
    ctx = ExitStack()
    with ctx:
        def sb(name, shape, dt=F32):
            return ctx.enter_context(nc.sbuf_tensor(name, shape, dt))

        def sem(name):
            return ctx.enter_context(nc.semaphore(name))

        bank = [ctx.enter_context(nc.psum_tensor(f"bank{b}", [P, 512], F32)) for b in range(8)]
        ring = sb("ring", [P, RING, SLOT])
        cs = sb("cs", [P, C_END])
        prow = sb("prow", [P, 5, P])
        gainT = sb("gainT", [P, G_END])
        convT = sb("convT", [P, 2, 4, 2, FT])
        gpost = sb("gpost", [P, 5, D])
        wr = sb("wr", [P, KT, NG + NE])
        br = sb("br", [P, NG + NE])
        lamp = sb("lamp", [P, 4, HD])
        h = sb("h", [P, NT, D])
        xn = sb("xn", [P, NT, D])
        xT = sb("xT", [P, KT, S])
        st = sb("st", [P, 64])
        att = sb("att", [P, 4, 2, 2, 2])
        room = sb("room", [P, 12800])

        def view(at, n):
            return room[:, at:at + n]

        def r3(ap, **k):
            return ap.rearrange("p (a b) -> p a b", **k)

        qT, kT = r3(view(0, 2048), b=S), r3(view(2048, 2048), b=S)
        vtok = r3(view(4096, 2048), b=D)
        oT = r3(view(6144, 2048), b=S)
        otok = r3(view(6144, 2048), b=D)
        qrT = r3(view(8192, 1024), b=S)
        krT = view(9216, 256)
        sc_sb = view(9472, 2048).rearrange("p (c j t k) -> p c j t k", c=2, j=2, t=NT)
        pT = view(11520, 1024).rearrange("p (c k q) -> p c k q", c=2, k=NT)
        scratch = view(12544, 256)
        pr_sb = xn[:, :, :].rearrange("p a (b c) -> p (a b) c", c=NT * S)
        cqn, ckvn = r3(view(0, 2 * QL), b=QL), r3(view(2048, NT * KVL), b=KVL)
        krr = r3(view(4096, NT * P), b=P)
        cqT, ckvT = r3(view(6144, 3 * S), b=S), r3(view(6144 + 3 * S, 2 * S), b=S)
        rt = r3(view(9472, 1536), b=512)
        rr = r3(view(11520, 1024), b=512)
        rr2 = rr.rearrange("p a (h d) -> p a h d", d=HD)
        qaT, kaT = r3(view(0, 1024), b=S), r3(view(1024, 1024), b=S)
        qbT, kbT = r3(view(2048, 1024), b=S), r3(view(3072, 1024), b=S)
        va, vb = r3(view(4096, 1024), b=512), r3(view(5120, 1024), b=512)
        oaT, obT = r3(view(6144, 1024), b=S), r3(view(7168, 1024), b=S)
        qiT, kiT = r3(view(8192, 1024), b=S), view(9216, 256)
        relu = r3(view(11520, 1024), b=NT * S)
        score = r3(view(6144, 512), b=S)
        work = [score, r3(view(6656, 512), b=S)]
        selm = r3(prow[:, 0:4, :].rearrange("p a b -> p (a b)"), b=S)
        siga, sigb = r3(view(0, 2048), b=D), r3(view(2048, 2048), b=D)
        mtmp = r3(view(4096, 2048), b=512)
        fbuf = [[view((6 * b + x) * S, S) for x in range(6)] for b in range(3)]
        cpar = view(18 * S, 48).rearrange("p (a b c) -> p a b c", a=4, b=2)
        mo = 0
        XgT = r3(view(0, KT * P), b=P)
        hid = view(1024, EF)
        silu = view(1536, EF)
        hidT = r3(view(2048, EF), b=P)
        ysb = view(2560, D)
        Sel = view(3584, NT * 2 * CAP).rearrange("p (t e c) -> p t e c", t=NT, e=2)
        SelG = view(3840, NT * 2 * CAP).rearrange("p (t e c) -> p t e c", t=NT, e=2)
        SgT = r3(view(4096, NT * P), b=P)
        gate, posm, mask = (r3(view(4352 + 64 * n, NT * NE), b=NE) for n in range(3))
        lg = r3(view(4608, NT * 36), b=36)
        rb = view(4700, 512)
        flag = sb("flag", [P, 1], I32)
        wi, top8 = sb("wi", [P, NT, 8]), sb("top8", [P, NT, 8])
        ss_o, rs_o = sb("ss_o", [P, 16]), sb("rs_o", [P, 16])
        w8 = rb[:, 0:8]
        r_top = [rb[:, 8 + 2 * n:10 + 2 * n] for n in range(5)]
        r_dif = [r3(rb[:, 24:32], b=NG), r3(rb[:, 32:48], b=EPG)]
        r_exp = [r3(rb[:, 48:56], b=NG), r3(rb[:, 56:72], b=EPG)]
        r_hot = [r3(rb[:, 72:80], b=NG), r3(rb[:, 80:96], b=EPG), r3(rb[:, 96:112], b=EPG)]
        r_sel = r3(rb[:, 112:128], b=EPG)
        r_prod = rb[:, 128:192].rearrange("p (t g e) -> p t g e", t=NT, g=NG)

        bank_full = [sem(f"bank_full{b}") for b in range(8)]
        bank_moved = [sem(f"bank_moved{b}") for b in range(8)]
        arrived = [sem(f"arrived{b}") for b in range(RING)]
        chunks_used = sem("chunks_used")
        s_const, s_rows, s_x, s_gains = sem("s_const"), sem("s_rows"), sem("s_x"), sem("s_gains")
        vec = sem("vec")
        h_ready, h_squares = sem("h_ready"), sem("h_squares")
        xn_ready = sem("xn_ready")
        down_squares, down_ready = sem("down_squares"), sem("down_ready")
        roped = sem("roped")
        post_squares = sem("post_squares")
        neg_max, exped, probs = sem("neg_max"), sem("exped"), sem("probs")
        o_ready, scored, mixed_ready = sem("o_ready"), sem("scored"), sem("mixed_ready")
        lam_dots, lam_exps = sem("lam_dots"), sem("lam_exps")
        up_full, centre, conv_done = sem("up_full"), sem("centre"), sem("conv_done")
        conv_step, g_squared, g_inner, tanhed, g_half, hid_ready = (
            sem(n) for n in ("conv_step", "g_squared", "g_inner", "tanhed", "g_half", "hid_ready"))
        params_set, ffn_full = sem("params_set"), sem("ffn_full")
        logits_max, logits_exp, mask_ready, flag_ready = (
            sem(n) for n in ("logits_max", "logits_exp", "mask_ready", "flag_ready"))
        sel_ready, selg_ready, xg_full, xg_ready, h1_full, h3_full, silu_ready, hidden_ready = (
            sem(n) for n in ("sel_ready", "selg_ready", "xg_full", "xg_ready", "h1_full", "h3_full",
                             "silu_ready", "hidden_ready"))
        hidT_full, hidT_ready, sgT_full, sgT_ready, y_full, y_ready, pos_step, moe_full = (
            sem(n) for n in ("hidT_full", "hidT_ready", "sgT_full", "sgT_ready", "y_full", "y_ready",
                             "pos_step", "moe_full"))
        out_ready, stored = sem("out_ready"), sem("stored")

        def full(eng, g):
            eng.wait_ge(bank_full[g % 8], g // 8 + 1)

        def moved(eng, g):
            eng.wait_ge(bank_moved[g % 8], g // 8 + 1)

        def slot(c, *shape):
            k, n = shape
            return ring[:, c % RING, 0:k * n].rearrange("p (k n) -> p k n", k=k)

        def have(eng, c, turn=0):
            eng.wait_ge(arrived[c % RING], 32 * (c // RING + 1) + 32 * turn)

        ident = cs[:, C_ID:C_ID + P]
        caus = r3(cs[:, C_CAUS:C_CAUS + NT * S], b=S)
        dist = r3(cs[:, C_DIST:C_DIST + NT * S], b=S)
        cos = r3(cs[:, C_COS:C_COS + NT * HD], b=HD)
        sin = r3(cs[:, C_SIN:C_SIN + NT * HD], b=HD)

        block = ctx.enter_context(nc.Block())

        @block.sync
        def _(sp):
            def load(c, parts, turn=0):
                if c >= RING:
                    sp.wait_ge(chunks_used, c - RING + 1 + RING * turn)
                for dst, src in parts:
                    sp.dma_start(dst, src).then_inc(arrived[c % RING], 16)

            def rows_cols(c, w, k, n):
                d, s = slot(c, k, n), w.rearrange("(k p) n -> p k n", p=P)
                a = k // 2
                load(c, [(d[:, :a], s[:, :a]), (d[:, a:], s[:, a:])])

            def rows_on(dst, src, n):
                sp.dma_start(dst, src.rearrange("(r m) -> r m", m=P)).then_inc(s_rows, 16)

            sp.dma_start(cs[:, :], cst).then_inc(s_const, 16)
            sp.dma_start(h[:, :, :], A["x"][0].rearrange("(t p) d -> p t d", p=P)).then_inc(s_x, 16)
            for n, src in enumerate([A["norm_g"][0, 0], A["norm_g"][0, 2], A["norm_g"][1, 0],
                                     A["norm_g"][1, 2], A["g_mix_2"][0], A["g_ffn_2"][0]]):
                rows_on(prow[8 * n:8 * n + 8, 0, :], src, 8)
            rows_on(prow[G_Q:G_Q + 3, 0, :], A["mla_q_norm_g"][0], 3)
            rows_on(prow[G_KV:G_KV + 2, 0, :], A["mla_kv_norm_g"][0], 2)
            rows_on(prow[G_SUB:G_SUB + 1, 0, :], A["diff_subln_g"][0], 1)
            for l in range(2):
                for w in range(2):
                    rows_on(prow[44 * w:44 * w + 44, 1 + 2 * l, :], A["ffn_conv_w"][l, w], 44)
                rows_on(prow[0:44, 2 + 2 * l, :], A["ffn_conv_w"][l, 2], 44)
                rows_on(prow[44:88, 2 + 2 * l, :], A["ffn_conv_b"][l], 44)

            rows_cols(C["dq"], A["mla_w_dq"][0], KT, QL)
            rows_cols(C["dkv"], A["mla_w_dkv"][0], KT, KVL + MR)
            for n in range(2):
                w = A["mla_w_uq"][0].rearrange("(k p) n -> p k n", p=P)[:, :, 768 * n:768 * n + 768]
                d = slot(C["uq"] + n, 3, 768)
                load(C["uq"] + n, [(d[:, :1], w[:, :1]), (d[:, 1:], w[:, 1:])])
            rows_cols(C["ukv"], A["mla_w_ukv"][0], 2, 2048)
            for n, (name, src) in enumerate([("norm_g", A["norm_g"][0, 1]), ("norm_g", A["norm_g"][0, 3]),
                                             ("norm_g", A["norm_g"][1, 1]), ("norm_g", A["norm_g"][1, 3]),
                                             ("g_final_2", A["g_final_2"])]):
                sp.dma_start(gpost[:, n, :], src.partition_broadcast(P)).then_inc(s_gains, 16)
            sp.dma_start(lamp[:, :, :].rearrange("p a b -> p (a b)"),
                         A["diff_lambda"][0].rearrange("a b -> (a b)").partition_broadcast(P)).then_inc(s_gains, 16)
            sp.dma_start(br[:, 0:NG], A["b_group_2"][0].partition_broadcast(P)).then_inc(s_gains, 16)
            sp.dma_start(br[:, NG:], A["b_expert_2"][0].partition_broadcast(P)).then_inc(s_gains, 16)
            sp.dma_start(wr[:, :, 0:NG], A["w_group_2"][0].rearrange("(k p) n -> p k n", p=P)).then_inc(s_gains, 16)
            sp.dma_start(wr[:, :, NG:], A["w_expert_2"][0].rearrange("(k p) n -> p k n", p=P)).then_inc(s_gains, 16)

            def square(c, w):
                for n in range(2):
                    rows_cols(c + n, w[512 * n:512 * n + 512, :], 4, D)

            def ffn_up(c, l, m, turn=0):
                w = A["ffn_w_up"][l].rearrange("(k p) (a n) -> p k a n", p=P, a=2)
                d = ring[:, c % RING, :].rearrange("p (k a n) -> p k a n", a=2, n=2 * P)
                load(c, [(d[:, :, a], w[:, :, a, bass.ds(m * 2 * P, 2 * P)]) for a in range(2)], turn)

            def ffn_down(c, l, m, turn=0):
                w = A["ffn_w_down"][l].rearrange("(k p) n -> p k n", p=P)
                d = slot(c, 2, D)
                load(c, [(d[:, x:x + 1], w[:, bass.ds(2 * m + x, 1)]) for x in range(2)], turn)

            def ffn(l):
                b = C[f"ffn{l}"]
                ffn_up(b, l, 0)
                ffn_up(b + 1, l, 1)
                ffn_down(b + 2, l, 0)
                with sp.Fori(0, 3) as i:
                    for s in range(3):
                        ffn_up(b + 3 + 2 * s, l, 3 * i + (2 + s), i)
                        ffn_down(b + 4 + 2 * s, l, 3 * i + (1 + s), i)
                ffn_down(b + 21, l, 10)

            square(C["mla_wo"], A["mla_w_o"][0])
            ffn(0)
            for n in range(6):
                rows_cols(C["qkv"] + n, A["diff_w_qkv"][0][:, 512 * n:512 * n + 512], KT, 512)
            square(C["diff_wo"], A["diff_w_o"][0])
            ffn(1)
            w_in = A["w_in_2"][0]
            for name, at, n in [("qi", 3072, 512), ("ki", 3584, 72), ("qa", 0, 512), ("ka", 512, 512),
                                ("va", 1024, 512), ("qb", 1536, 512), ("kb", 2048, 512), ("vb", 2560, 512)]:
                rows_cols(C[name], w_in[:, at:at + n], KT, n)
            for n in range(4):
                rows_cols(C["gates"] + n, w_in[:, 3656 + 512 * n:4168 + 512 * n], KT, 512)
            rows_cols(C["pa"], A["w_proj_a_2"][0], 4, D)
            rows_cols(C["pb"], A["w_proj_b_2"][0], 4, D)
            square(C["wout"], A["w_out_2"][0])

            def pair(i, turn):
                c = C["moe"]
                for x, (name, k, n) in enumerate([("w1_2", KT, EF), ("w3_2", KT, EF), ("w2_2", 4, D)]):
                    for e in range(2):
                        w = A[name][0].rearrange("e (k p) n -> p e k n", p=P)
                        d = slot(c + 2 * x + e, k, n)
                        load(c + 2 * x + e,
                             [(d[:, a * k // 2:(a + 1) * k // 2],
                               w[:, bass.ds(2 * i + e, 1), a * k // 2:(a + 1) * k // 2, :].rearrange(
                                   "p e k n -> p (e k) n")) for a in range(2)], turn)

            with sp.Fori(0, NP) as i:
                pair(i, i)
            sp.wait_ge(flag_ready, 1)
            over = sp.value_load(flag[0:1, 0:1], min_val=0, max_val=1)
            with sp.If(over):
                with sp.Fori(1, ROUNDS) as r:
                    with sp.Fori(0, NP) as i:
                        pair(i, r * NP + i)
            sp.wait_ge(out_ready, NT)
            sp.dma_start(out[0].rearrange("(t p) d -> p t d", p=P), xn[:, :, :]).then_inc(stored, 16)
            sp.wait_ge(stored, 16)

        @block.tensor
        def _(pe):
            def begin(g):
                if g >= 8:
                    moved(pe, g - 8)
                return bank[g % 8]

            def end(ins, g):
                ins.then_inc(bank_full[g % 8], 1)

            def used(ins):
                ins.then_inc(chunks_used, 1)

            def transposes(g, blocks, frees=0):
                b = begin(g)
                at = 0
                for n, src in enumerate(blocks):
                    rows, cols = src.shape[0], src.shape[1]
                    ins = pe.transpose(b[0:cols, at:at + rows], src, ident[0:rows, 0:rows])
                    if n == 0 and frees:
                        ins.then_inc(chunks_used, frees)
                    at += rows
                end(ins, g)

            def x_transposed(name, site):
                for t in range(NT):
                    pe.wait_ge(xn_ready, 2 * site + t + 1)
                    for q in range(2):
                        transposes(G[name] + 2 * t + q,
                                   [xn[:, t, P * k:P * k + P] for k in range(4 * q, 4 * q + 4)],
                                   frees=int(site > 0 and t == 0 and q == 0))
                for g in range(4):
                    moved(pe, G[name] + g)

            def by_token(g, t, x, w, cols, kt, frees=0):
                b = begin(g)
                for k in range(kt):
                    o = b[:, 0:cols] if len(w[:, k].shape) == 2 else b[:, 0:cols].rearrange(
                        "p (a b) -> p a b", b=w.shape[-1])
                    ins = pe.matmul(o, x[:, k, t * P:t * P + P], w[:, k], start=k == 0, stop=k == kt - 1)
                    if k == 0 and frees:
                        ins.then_inc(chunks_used, frees)
                end(ins, g)

            def by_feature(g, ws, x, kt, frees=0):
                b = begin(g)
                for n, w in enumerate(ws):
                    for k in range(kt):
                        ins = pe.matmul(b[:, n * S:n * S + S], w[:, k], x[:, k, :], start=k == 0, stop=k == kt - 1)
                        if n == 0 and k == 0 and frees:
                            ins.then_inc(chunks_used, frees)
                end(ins, g)

            def square_out(g0, c0, x, frees=0):
                for n in range(2):
                    have(pe, c0 + n)
                    w = slot(c0 + n, 4, D)
                    for t in range(NT):
                        for hf in range(2):
                            g = g0 + 2 * t + hf
                            b = begin(g) if n == 0 else bank[g % 8]
                            for k in range(4):
                                ins = pe.matmul(b[:, :], x[:, 4 * n + k, t * P:t * P + P],
                                                w[:, k, 512 * hf:512 * hf + 512],
                                                start=n == 0 and k == 0, stop=n == 1 and k == 3)
                                if t == 0 and hf == 0 and k == 0 and (n or frees):
                                    ins.then_inc(chunks_used, 1 if n else frees)
                            if n == 1:
                                end(ins, g)

            def attention(base, heads, maps, q_of, k_of, values, by_tokens, ready, o_ok=None):
                sc, tr, ou, _ = attention_groups(base, heads, maps)
                for g in ready:
                    moved(pe, g)
                for s in range(heads + 2):
                    if s < heads:
                        for j in range(maps):
                            b = begin(sc[s, j])
                            for t in range(NT):
                                qs, ks = q_of(s, j), k_of(s, j)
                                for n in range(len(qs)):
                                    ins = pe.matmul(b[:, t * S:t * S + S], qs[n][:, t * P:t * P + P], ks[n],
                                                    start=n == 0, stop=n == len(qs) - 1)
                            end(ins, sc[s, j])
                    if 1 <= s <= heads:
                        hd = s - 1
                        pe.wait_ge(probs, att_done[0] + hd + 1)
                        b = begin(tr[hd])
                        for k in range(NT):
                            for t in range(NT):
                                ins = pe.transpose(b[:, k * S + t * P:k * S + t * P + P],
                                                   pr_sb[:, 2 * (hd % 2), t * S + k * P:t * S + k * P + P], ident)
                        end(ins, tr[hd])
                    if s >= 2:
                        hd = s - 2
                        moved(pe, tr[hd])
                        b = begin(ou[hd])
                        if by_tokens:
                            for t in range(NT):
                                for k in range(NT):
                                    ins = pe.matmul(b[:, t * P:t * P + P], pT[:, hd % 2, k, t * P:t * P + P],
                                                    values(hd, k), start=k == 0, stop=k == NT - 1)
                        else:
                            v = [values(hd, k) for k in range(NT)]
                            m = v[0].shape[1]
                            at = 64 * (hd % 2) if m == 64 else 0
                            for k in range(NT):
                                ins = pe.matmul(b[at:at + m, 0:S], v[k], pT[:, hd % 2, k, :],
                                                start=k == 0, stop=k == NT - 1)
                        end(ins, ou[hd])
                att_done[0] += heads

            att_done = [0]

            pe.wait_ge(s_const, 16)
            pe.wait_ge(s_rows, 17 * 16)
            transposes(G["par"], [prow[0:G_END, 0, :]])
            for l in range(2):
                transposes(G["par"] + 1 + l, [prow[0:88, 1 + 2 * l, :], prow[0:88, 2 + 2 * l, :]])

            x_transposed("x0", 0)
            g = G["mla_down"]
            have(pe, C["dq"])
            for t in range(NT):
                by_token(g + t, t, xT, slot(C["dq"], KT, QL), QL, KT)
            have(pe, C["dkv"])
            for t in range(NT):
                by_token(g + 2 + t, t, xT, slot(C["dkv"], KT, KVL + MR), KVL + MR, KT, frees=int(t == 0))
            for t in range(NT):
                pe.wait_ge(down_ready, t + 1)
                transposes(G["mla_t"] + t, [cqn[:, t, P * k:P * k + P] for k in range(3)], frees=int(t == 0))
            for t in range(NT):
                transposes(G["mla_t2"] + t, [ckvn[:, t, P * k:P * k + P] for k in range(2)] + [krr[:, t, :]])
            for t in range(NT):
                moved(pe, G["mla_t"] + t)
            uq = [slot(C["uq"] + n, 3, 768).rearrange("p k (h d) -> p k h d", d=MN + MR) for n in range(2)]
            for n in range(2):
                have(pe, C["uq"] + n)
                for x in range(2):
                    by_feature(G["mla_qn"] + 2 * n + x, [uq[n][:, :, 2 * x + y, 0:MN] for y in range(2)], cqT, 3)
            for t in range(NT):
                b = begin(G["mla_qr"] + t)
                for n in range(2):
                    for k in range(3):
                        ins = pe.matmul(b[:, S * n:S * n + S].rearrange("p (h d) -> p h d", d=MR),
                                        cqT[:, k, t * P:t * P + P], uq[n][:, k, :, MN:],
                                        start=k == 0, stop=k == 2)
                end(ins, G["mla_qr"] + t)
            for t in range(NT):
                moved(pe, G["mla_t2"] + t)
            have(pe, C["ukv"])
            ukv = slot(C["ukv"], 2, 2048).rearrange("p k (h d) -> p k h d", d=2 * MN)
            for x in range(4):
                by_feature(G["mla_kn"] + x, [ukv[:, :, 2 * x + y, 0:MN] for y in range(2)], ckvT, 2,
                           frees=2 * (x == 0))
            for t in range(NT):
                for hf in range(2):
                    by_token(G["mla_v"] + 2 * t + hf, t, ckvT, ukv[:, :, 4 * hf:4 * hf + 4, MN:], 512, 2)
            for t in range(NT):
                pe.wait_ge(roped, t + 1)
                transposes(G["mla_qrt"] + t, [rr[:, t, P * k:P * k + P] for k in range(4)], frees=int(t == 0))
            attention(G["mla_att"], MH, 1,
                      lambda s, j: [qT[:, s, :], qrT[64 * (s % 2):64 * (s % 2) + 64, s // 2, :]],
                      lambda s, j: [kT[:, s, :], krT[64 * (s % 2):64 * (s % 2) + 64, :]],
                      lambda hd, k: vtok[:, k, P * hd:P * hd + P], False,
                      range(G["mla_qn"], G["mla_att"]))
            for hd in range(MH):
                moved(pe, attention_groups(G["mla_att"], MH, 1)[2][hd])
            square_out(G["mla_o"], C["mla_wo"], oT)

            def ffn(l):
                b = C[f"ffn{l}"]
                n0 = l * FT

                def up(c, x, j, j3, turn=0, frees=0):
                    if x == 0:
                        have(pe, c, turn)
                    w = ring[:, c % RING, :].rearrange("p (k a n) -> p k a n", a=2, n=2 * P)
                    for a in range(2):
                        for k in range(KT):
                            ins = pe.matmul(bank[j3][:, a * S:a * S + S], w[:, k, a, P * x:P * x + P], xT[:, k, :],
                                            start=k == 0, stop=k == KT - 1)
                            if a == 0 and k == 0 and frees:
                                ins.then_inc(chunks_used, frees)
                    ins.then_inc(up_full, 1)

                def down(c, x, j, j3, turn=0, frees=0, first=False, last=False):
                    if x == 0:
                        have(pe, c, turn)
                    pe.wait_ge(hid_ready, n0 + 1 + j)
                    w = slot(c, 2, D)
                    for t in range(NT):
                        for hf in range(2):
                            ins = pe.matmul(bank[4 + 2 * t + hf][:, :], fbuf[j3][4][:, t * P:t * P + P],
                                            w[:, x, 512 * hf:512 * hf + 512], start=first, stop=last)
                            if t == 0 and hf == 0 and frees:
                                ins.then_inc(chunks_used, frees)
                    if last:
                        ins.then_inc(ffn_full, 1)

                up(b, 0, 0, 0)
                up(b, 1, 1, 1)
                up(b + 1, 0, 2, 2, frees=1)
                down(b + 2, 0, 0, 0, first=True)
                up(b + 1, 1, 3, 0)
                down(b + 2, 1, 1, 1, frees=1)
                with pe.Fori(0, 3) as i:
                    for s in range(3):
                        j = 4 + 2 * s
                        up(b + 3 + 2 * s, 0, j, j % 3, i, frees=1)
                        down(b + 4 + 2 * s, 0, 6 * i + (j - 2), (j - 2) % 3, i)
                        up(b + 3 + 2 * s, 1, j + 1, (j + 1) % 3, i)
                        down(b + 4 + 2 * s, 1, 6 * i + (j - 1), (j - 1) % 3, i, frees=1)
                down(b + 21, 0, FT - 2, (FT - 2) % 3, frees=1)
                down(b + 21, 1, FT - 1, (FT - 1) % 3, last=True)

            x_transposed("x1", 1)
            ffn(0)

            x_transposed("x2", 2)
            for n in range(2):
                for hf in range(2):
                    c = C["qkv"] + 2 * n + hf
                    have(pe, c)
                    w = slot(c, KT, 512)
                    for x in range(2):
                        by_feature(G["diff_q"] + 4 * n + 2 * hf + x,
                                   [w[:, :, 256 * x + P * y:256 * x + P * y + P] for y in range(2)], xT, KT,
                                   frees=int(x == 0 and n + hf > 0))
            for hf in range(2):
                c = C["qkv"] + 4 + hf
                have(pe, c)
                for t in range(NT):
                    by_token(G["diff_v"] + 2 * hf + t, t, xT, slot(c, KT, 512), 512, KT, frees=int(t == 0))
            attention(G["diff_att"], DH, 2,
                      lambda s, j: [qT[64 * j:64 * j + 64, s, :]], lambda s, j: [kT[64 * j:64 * j + 64, s, :]],
                      lambda hd, k: vtok[:, k, P * hd:P * hd + P], True,
                      range(G["diff_q"], G["diff_att"]))
            for t in range(NT):
                pe.wait_ge(o_ready, t + 1)
                for q in range(2):
                    transposes(G["diff_t"] + 2 * t + q, [otok[:, t, P * k:P * k + P] for k in range(4 * q, 4 * q + 4)],
                               frees=int(t == 0 and q == 0))
            for g in range(4):
                moved(pe, G["diff_t"] + g)
            square_out(G["diff_o"], C["diff_wo"], xT)
            x_transposed("x3", 3)
            ffn(1)

            x_transposed("x4", 4)
            n_rot = [NT]

            def rotated(name, cols, frees=1):
                c = C[name]
                have(pe, c)
                for t in range(NT):
                    by_token(G[name] + t, t, xT, slot(c, KT, cols), cols, KT, frees=frees * (t == 0))
                for t in range(NT):
                    pe.wait_ge(roped, n_rot[0] + t + 1)
                    transposes(G[name + "_t"] + t, [rr[:, t, P * k:P * k + P] for k in range(4 if cols == 512 else 1)])
                n_rot[0] += NT

            rotated("qi", 512, frees=0)
            rotated("ki", 72)
            for g in range(G["qi_t"], G["qi_t"] + 2):
                moved(pe, g)
            for g in range(G["ki_t"], G["ki_t"] + 2):
                moved(pe, g)
            for hd in range(8):
                b = begin(G["index"] + hd)
                at = 64 * (hd % 2)
                for t in range(NT):
                    ins = pe.matmul(b[:, t * S:t * S + S], qiT[at:at + 64, hd // 2, t * P:t * P + P],
                                    kiT[at:at + 64, :], start=True, stop=True)
                end(ins, G["index"] + hd)

            def values(name):
                have(pe, C[name])
                for t in range(NT):
                    by_token(G[name] + t, t, xT, slot(C[name], KT, 512), 512, KT, frees=int(t == 0))

            for a in "ab":
                rotated("q" + a, 512)
                rotated("k" + a, 512)
                values("v" + a)

            def halves(ap):
                return lambda s, j: [ap[64 * (s % 2):64 * (s % 2) + 64, s // 2, :]]

            for name, q_, k_, v_, a in [("moba_att", qaT, kaT, va, "a"), ("dsa_att", qbT, kbT, vb, "b")]:
                attention(G[name], 8, 1, halves(q_), halves(k_),
                          lambda hd, k, v_=v_: v_[:, k, 64 * hd:64 * hd + 64], False,
                          [*range(G["q" + a + "_t"], G["q" + a + "_t"] + 2),
                           *range(G["k" + a + "_t"], G["k" + a + "_t"] + 2), *range(G["v" + a], G["v" + a] + 2)])
            for n in range(4):
                have(pe, C["gates"] + n)
                for t in range(NT):
                    by_token(G["gates"] + 2 * n + t, t, xT, slot(C["gates"] + n, KT, 512), 512, KT, frees=int(t == 0))
            for name, x, att_name in [("pa", oaT, "moba_att"), ("pb", obT, "dsa_att")]:
                for hd in range(8):
                    moved(pe, attention_groups(G[att_name], 8, 1)[2][hd])
                have(pe, C[name])
                w = slot(C[name], 4, D)
                for t in range(NT):
                    for hf in range(2):
                        by_token(G[name] + 2 * t + hf, t, x, w[:, :, 512 * hf:512 * hf + 512], 512, 4,
                                 frees=int(t == 0 and hf == 0))
            for t in range(NT):
                pe.wait_ge(mixed_ready, t + 1)
                for q in range(2):
                    transposes(G["mix_t"] + 2 * t + q, [siga[:, t, P * k:P * k + P] for k in range(4 * q, 4 * q + 4)],
                               frees=int(t == 0 and q == 0))
            for g in range(4):
                moved(pe, G["mix_t"] + g)
            square_out(G["hyb_o"], C["wout"], xT)

            x_transposed("x5", 5)
            pe.wait_ge(s_gains, 16 * 10)
            for t in range(NT):
                by_token(G["router"] + t, t, xT, wr, NG + NE, KT)
            pe.wait_ge(mask_ready, 1)
            b = begin(G["pos"])
            tri, one, zero = (cs[:, c:c + P] for c in (C_TRI, C_ONE, C_ZERO))
            pe.matmul(b[:, 0:NE], tri, mask[:, 0, :], start=True, stop=True)
            pe.matmul(b[:, NE:2 * NE], one, mask[:, 0, :], start=True, stop=False)
            pe.matmul(b[:, NE:2 * NE], tri, mask[:, 1, :], start=False, stop=True)
            pe.matmul(b[:, 2 * NE:3 * NE], one, mask[:, 0, :], start=True, stop=False)
            end(pe.matmul(b[:, 2 * NE:3 * NE], one, mask[:, 1, :], start=False, stop=True), G["pos"])

            moved(pe, G["pos"])
            for b in range(4, 8):
                pe.matmul(bank[b][:, :], zero, cs[:, 0:512], start=True, stop=False)

            def gather(n, first=0, last=KT, frees=0):
                if first == 0:
                    pe.wait_ge(sel_ready, 1 + n)
                for k in range(first, last):
                    for t in range(NT):
                        ins = pe.matmul(bank[2 + k // 4][:, P * (k % 4):P * (k % 4) + P],
                                        xn[:, t, P * k:P * k + P], Sel[:, t].rearrange("p e c -> p (e c)"),
                                        start=t == 0, stop=t == NT - 1)
                        if k == 0 and t == 0 and frees:
                            ins.then_inc(chunks_used, frees)
                if last == KT:
                    ins.then_inc(xg_full, 1)

            def scatter(n, frees=0):
                pe.wait_ge(sgT_ready, 1 + n)
                pe.wait_ge(y_ready, 2 + 2 * n)
                for t in range(NT):
                    for hf in range(2):
                        ins = pe.matmul(bank[4 + 2 * t + hf][:, :], SgT[:, t, :], ysb[:, 512 * hf:512 * hf + 512],
                                        start=False, stop=False)
                        if t == 0 and hf == 0 and frees:
                            ins.then_inc(chunks_used, frees)

            def pair(n, turn, first=False, opens=False, last=False):
                c = C["moe"]
                pe.wait_ge(xg_ready, 2 + 2 * n)
                if not first:
                    pe.wait_ge(y_ready, 2 * n)
                    pe.wait_ge(sgT_ready, n)
                for x, done in enumerate((h1_full, h3_full)):
                    have(pe, c + 2 * x, turn)
                    have(pe, c + 2 * x + 1, turn)
                    for k in range(KT):
                        for e in range(2):
                            ins = pe.matmul(bank[x][CAP * e:CAP * e + CAP, :], XgT[:, k, CAP * e:CAP * e + CAP],
                                            slot(c + 2 * x + e, KT, EF)[:, k, :], start=k == 0, stop=k == KT - 1)
                            if k == 0 and e == 0 and (x or not first):
                                ins.then_inc(chunks_used, 2)
                    ins.then_inc(done, 1)
                if not opens:
                    scatter(n - 1, frees=2)
                if not last:
                    gather(n + 1, 0, 6, frees=2 * opens)
                pe.wait_ge(hidden_ready, 1 + n)
                for k in range(4):
                    ins = pe.transpose(bank[0][:, P * k:P * k + P], hid[:, P * k:P * k + P], ident)
                ins.then_inc(hidT_full, 1)
                if not last:
                    gather(n + 1, 6, KT)
                pe.wait_ge(hidT_ready, 1 + n)
                have(pe, c + 4, turn)
                have(pe, c + 5, turn)
                for hf in range(2):
                    if hf == 1:
                        pe.wait_ge(selg_ready, 1 + n)
                        for t in range(NT):
                            ins = pe.transpose(bank[0][:, P * t:P * t + P],
                                               SelG[:, t].rearrange("p e c -> p (e c)"), ident)
                        ins.then_inc(sgT_full, 1)
                        if not last:
                            pe.wait_ge(xg_ready, 4 + 2 * n)
                    for k in range(4):
                        for e in range(2):
                            ins = pe.matmul(bank[1 + hf][CAP * e:CAP * e + CAP, :], hidT[:, k, CAP * e:CAP * e + CAP],
                                            slot(c + 4 + e, 4, D)[:, k, 512 * hf:512 * hf + 512],
                                            start=k == 0, stop=k == 3)
                    ins.then_inc(y_full, 1)

            gather(0)
            pair(0, 0, first=True, opens=True)
            with pe.Fori(1, NP - 1) as i:
                pair(i, i)
            pair(NP - 1, NP - 1, last=True)
            scatter(NP - 1)
            pe.wait_ge(flag_ready, 1)
            over = pe.value_load(flag[0:1, 0:1], min_val=0, max_val=1)
            with pe.If(over):
                with pe.Fori(1, ROUNDS) as r:
                    gather(r * NP)
                    pair(r * NP, r * NP, opens=True)
                    with pe.Fori(1, NP - 1) as i:
                        pair(r * NP + i, r * NP + i)
                    pair(r * NP + (NP - 1), r * NP + (NP - 1), last=True)
                    scatter(r * NP + (NP - 1))
            for b in range(4, 8):
                ins = pe.matmul(bank[b][:, :], zero, cs[:, 0:512], start=False, stop=True)
            ins.then_inc(moe_full, 1)

        @block.scalar
        def _(act):
            def squares(dst, src, junk, done):
                act.activation(junk, src, ACT.Square, accum_out=dst).then_inc(done, 1)

            def h_sums(site):
                for t in range(NT):
                    if site == 0:
                        act.wait_ge(s_x, 16)
                    else:
                        act.wait_ge(h_ready, 2 * (site - 1) + t + 1)
                    squares(st[:, t:t + 1], h[:, t, :], xn[:, t, :], h_squares)

            def copy(g, dst, src, func=ACT.Copy, scale=1.0):
                full(act, g)
                act.activation(dst, src, func, scale=scale).then_inc(bank_moved[g % 8], 1)

            def out_sums(banks):
                for n, (b, wait) in enumerate(banks):
                    wait(act)
                    squares(st[:, 2 + n:3 + n], bank[b][:, :], xn[:, n // 2, 512 * (n % 2):512 * (n % 2) + 512],
                            post_squares)

            def group_banks(g0):
                return [((g0 + n) % 8, lambda e, g=g0 + n: full(e, g)) for n in range(4)]

            def ffn_banks(l):
                return [(4 + n, lambda e: e.wait_ge(ffn_full, l + 1)) for n in range(4)]

            heads_done, exps_done = [0], [0]

            def attention(base, heads, maps, scale, biased, outputs):
                sc, tr, ou, _ = attention_groups(base, heads, maps)
                for s in range(heads + 2):
                    c = s % 2
                    if s < heads:
                        act.wait_ge(neg_max, heads_done[0] + s + 1)
                        for j in range(maps):
                            for t in range(NT):
                                src = sc_sb[:, c, j, t, :] if biased else bank[sc[s, 0] % 8][:, t * S:t * S + S]
                                ins = act.activation(pr_sb[:, 2 * c + j, t * S:t * S + S], src, ACT.Exp,
                                                     bias=att[:, 1, c, j, t:t + 1], scale=scale,
                                                     accum_out=att[:, 2, c, j, t:t + 1])
                                if biased:
                                    ins.then_inc(exped, 1)
                                elif t == NT - 1:
                                    ins.then_inc(bank_moved[sc[s, 0] % 8], 1)
                    if s >= 2:
                        g = ou[s - 2]
                        dst, src = outputs(s - 2, bank[g % 8])
                        copy(g, dst, src)
                heads_done[0] += heads

            h_sums(0)
            for t in range(NT):
                full(act, G["mla_down"] + t)
                squares(st[:, 6 + t:7 + t], bank[(G["mla_down"] + t) % 8][:, 0:QL], view(8192 + QL * t, QL), down_squares)
            for t in range(NT):
                full(act, G["mla_down"] + 2 + t)
                squares(st[:, 8 + t:9 + t], bank[(G["mla_down"] + 2 + t) % 8][:, 0:KVL],
                        view(8192 + 2 * QL + KVL * t, KVL), down_squares)
            for x in range(4):
                g = G["mla_qn"] + x
                copy(g, view(512 * x, 512), bank[g % 8][:, :])
            for x in range(4):
                g = G["mla_kn"] + x
                copy(g, view(2048 + 512 * x, 512), bank[g % 8][:, :])
            for x in range(4):
                g = G["mla_v"] + x
                copy(g, view(4096 + 512 * x, 512), bank[g % 8][:, :])

            def tiles(g, dst, t, n, **k):
                copy(g, dst[:, 0:n, t * P:t * P + P], bank[g % 8][:, 0:n * P].rearrange("p (a b) -> p a b", b=P), **k)

            for t in range(NT):
                tiles(G["mla_qrt"] + t, qrT, t, 4)
            attention(G["mla_att"], MH, 1, MLA_SCALE, False, lambda hd, b: (oT[:, hd, :], b[:, 0:S]))
            out_sums(group_banks(G["mla_o"]))

            def tile(n, b, par):
                act.wait_ge(up_full, 1 + n)
                for a in range(2):
                    act.activation(fbuf[b][a], bank[b][:, a * S:a * S + S], ACT.Identity,
                                   bias=par(3, a), scale=par(1, a)).then_inc(centre, 1)
                act.wait_ge(conv_done, 1 + n)
                act.activation(fbuf[b][2], fbuf[b][0], ACT.Square, scale=0.044715 ** 0.5).then_inc(g_squared, 1)
                act.wait_ge(g_inner, 1 + n)
                act.activation(fbuf[b][5], fbuf[b][3], ACT.Tanh, scale=(2 / np.pi) ** 0.5).then_inc(tanhed, 1)

            def ffn(l):
                for j in range(4):
                    tile(l * FT + j, j % 3, lambda w, a: convT[:, l, w, a, j:j + 1])
                with act.Fori(0, 3) as i:
                    act.wait_ge(params_set, i + (3 * l + 1))
                    for x in range(6):
                        tile(6 * i + (l * FT + 4 + x), (4 + x) % 3, lambda w, a: cpar[:, w, a, x:x + 1])

            h_sums(1)
            ffn(0)
            out_sums(ffn_banks(0))

            h_sums(2)
            act.wait_ge(lam_dots, 1)
            act.activation(st[:, 12:14], st[:, 10:12], ACT.Exp).then_inc(lam_exps, 1)
            for x in range(8):
                g = G["diff_q"] + x
                copy(g, view(512 * x, 512), bank[g % 8][:, :])
            for hf in range(2):
                for t in range(NT):
                    g = G["diff_v"] + 2 * hf + t
                    copy(g, vtok[:, t, 512 * hf:512 * hf + 512], bank[g % 8][:, :])
            attention(G["diff_att"], DH, 2, HD_SCALE, True,
                      lambda hd, b: (otok[:, :, P * hd:P * hd + P], b[:, 0:S].rearrange("p (t d) -> p t d", t=NT)))
            act.wait_ge(o_ready, 1)
            for t in range(NT):
                for q in range(2):
                    tiles(G["diff_t"] + 2 * t + q, xT[:, 4 * q:4 * q + 4], t, 4, scale=st[:, 15:16])
            out_sums(group_banks(G["diff_o"]))
            h_sums(3)
            ffn(1)
            out_sums(ffn_banks(1))

            h_sums(4)
            for t in range(NT):
                tiles(G["qi_t"] + t, qiT, t, 4)
            for t in range(NT):
                g = G["ki_t"] + t
                copy(g, kiT[:, t * P:t * P + P], bank[g % 8][:, 0:P])
            for hd in range(8):
                if hd >= 2:
                    act.wait_ge(scored, hd - 1)
                g = G["index"] + hd
                full(act, g)
                act.activation(relu[:, hd % 2, :], bank[g % 8][:, :], ACT.Relu).then_inc(bank_moved[g % 8], 1)
            for a, q_, k_, v_ in [("a", qaT, kaT, va), ("b", qbT, kbT, vb)]:
                for name, dst in [("q", q_), ("k", k_)]:
                    for t in range(NT):
                        tiles(G[name + a + "_t"] + t, dst, t, 4)
                for t in range(NT):
                    g = G["v" + a] + t
                    copy(g, v_[:, t, :], bank[g % 8][:, :])
            for name, dst in [("moba_att", oaT), ("dsa_att", obT)]:
                attention(G[name], 8, 1, HD_SCALE, True,
                          lambda hd, b, dst=dst: (dst[64 * (hd % 2):64 * (hd % 2) + 64, hd // 2, :],
                                                  b[64 * (hd % 2):64 * (hd % 2) + 64, 0:S]))
            for n in range(4):
                for t in range(NT):
                    g = G["gates"] + 2 * n + t
                    copy(g, (siga, sigb)[n // 2][:, t, 512 * (n % 2):512 * (n % 2) + 512], bank[g % 8][:, :], ACT.Sigmoid)
            for t in range(NT):
                for q in range(2):
                    tiles(G["mix_t"] + 2 * t + q, xT[:, 4 * q:4 * q + 4], t, 4)
            h_sums(5)

            for n in range(2):
                act.wait_ge(logits_max, n + 1)
                act.activation(r_exp[n], r_dif[n], ACT.Exp).then_inc(logits_exp, 1)

            def pair(n):
                act.wait_ge(h1_full, 1 + n)
                act.activation(silu, bank[0][:, :], ACT.Silu).then_inc(silu_ready, 1)
                act.wait_ge(hidT_full, 1 + n)
                act.activation(hidT.rearrange("p a b -> p (a b)"), bank[0][:, :], ACT.Copy).then_inc(hidT_ready, 1)
                for hf in range(2):
                    act.wait_ge(y_full, 2 * n + (1 + hf))
                    act.activation(ysb[:, 512 * hf:512 * hf + 512], bank[1 + hf][:, :], ACT.Copy).then_inc(y_ready, 1)

            with act.Fori(0, NP) as i:
                pair(i)
            act.wait_ge(flag_ready, 1)
            over = act.value_load(flag[0:1, 0:1], min_val=0, max_val=1)
            with act.If(over):
                with act.Fori(NP, ROUNDS * NP) as n:
                    pair(n)
            h_sums(6)

        @block.vector
        def _(dve):
            steps = [0]

            def link(ins):
                steps[0] += 1
                ins.then_inc(vec, 1)
                dve.wait_ge(vec, steps[0])

            def rsqrt(dst, src, n, scale):
                v, a = st[:, 32:32 + n], st[:, 48:48 + n]
                link(dve.tensor_scalar(v, src, scale, EPS, ALU.mult, ALU.add))
                link(dve.tensor_scalar(a.bitcast(I32), v.bitcast(I32), 1, None, ALU.arith_shift_right))
                link(dve.tensor_scalar(dst.bitcast(I32), a.bitcast(I32), -1, 0x5f3759df, ALU.mult, ALU.add))
                for _ in range(4):
                    link(dve.tensor_tensor(a, dst, dst, ALU.mult))
                    link(dve.scalar_tensor_tensor(a, a, -0.5, v, ALU.mult, ALU.mult))
                    link(dve.scalar_tensor_tensor(dst, a, 1.5, dst, ALU.add, ALU.mult))

            def spread(ap, *shape):
                return ap.unsqueeze(len(ap.shape)).to_broadcast([P, *shape])

            def blocks(ap, n):
                return ap[:, 0:n * P].rearrange("p (a b) -> p a b", b=P)

            def gained(g, dst, src, col, n, moves=True):
                ins = dve.tensor_tensor(dst, src, spread(gainT[:, col:col + n], n, P), ALU.mult)
                if moves:
                    ins.then_inc(bank_moved[g % 8], 1)

            def normed(site):
                dve.wait_ge(h_squares, 2 * site + 2)
                rsqrt(st[:, 16:18], st[:, 0:2], 2, 1.0 / D)
                for t in range(NT):
                    dve.tensor_scalar(xn[:, t, :], h[:, t, :], st[:, 16 + t:17 + t], None, ALU.mult).then_inc(xn_ready, 1)

            def x_transposed(name, site):
                normed(site)
                for t in range(NT):
                    for q in range(2):
                        g = G[name] + 2 * t + q
                        full(dve, g)
                        gained(g, xT[:, 4 * q:4 * q + 4, t * P:t * P + P], blocks(bank[g % 8], 4), G_N[site] + 4 * q, 4)

            def post(site, banks, ring_groups):
                dve.wait_ge(post_squares, 4 * site + 4)
                link(dve.tensor_tensor(st[:, 18:20], st[:, 2:6].rearrange("p (t h) -> p t h", h=2)[:, :, 0],
                                       st[:, 2:6].rearrange("p (t h) -> p t h", h=2)[:, :, 1], ALU.add))
                rsqrt(st[:, 16:18], st[:, 18:20], 2, 1.0 / D)
                for n, b in enumerate(banks):
                    t, hf = divmod(n, 2)
                    ins = dve.scalar_tensor_tensor(xn[:, t, 512 * hf:512 * hf + 512], bank[b][:, :], st[:, 16 + t:17 + t],
                                                   gpost[:, site, 512 * hf:512 * hf + 512], ALU.mult, ALU.mult)
                    ins.then_inc(bank_moved[b] if ring_groups else vec, 1)
                if ring_groups:
                    for g in ring_groups:
                        moved(dve, g)
                else:
                    steps[0] += 4
                    dve.wait_ge(vec, steps[0])
                for t in range(NT):
                    dve.tensor_tensor(h[:, t, :], h[:, t, :], xn[:, t, :], ALU.add).then_inc(h_ready, 1)

            rotations = {}

            def rope(g, t, nh, dst=None, done=roped, off=0):
                if rotations:
                    last = rotations["last"]
                    dve.wait_ge(last, rotations[last.name])
                rotations[done.name] = rotations.get(done.name, 0) + 1
                rotations["last"] = done
                src = bank[g % 8][:, off:off + nh * HD].rearrange("p (h two d) -> p h two d", two=2, d=32)
                t1 = rt[:, 0, 0:nh * HD].rearrange("p (h d) -> p h d", d=HD)
                t2 = rt[:, 1, 0:nh * HD].rearrange("p (h two d) -> p h two d", two=2, d=32)
                cb = cos[:, t, :].unsqueeze(1).to_broadcast([P, nh, HD])
                dve.tensor_tensor(t1, bank[g % 8][:, off:off + nh * HD].rearrange("p (h d) -> p h d", d=HD), cb, ALU.mult)
                for y in range(2):
                    sb_ = sin[:, t, 32 * y:32 * y + 32].unsqueeze(1).to_broadcast([P, nh, 32])
                    ins = dve.tensor_tensor(t2[:, :, y, :], src[:, :, 1 - y, :], sb_, ALU.mult)
                ins.then_inc(bank_moved[g % 8], 1)
                moved(dve, g)
                if dst is None:
                    dve.tensor_tensor(rr[:, t, 0:nh * HD], rt[:, 0, 0:nh * HD], rt[:, 1, 0:nh * HD],
                                      ALU.add).then_inc(roped, 1)
                else:
                    a, b = (rt[:, y, 0:HD].unsqueeze(1).to_broadcast([P, 2, HD]) for y in range(2))
                    dve.tensor_tensor(dst, a, b, ALU.add).then_inc(done, 1)

            heads_done, exps_done = [0], [0]

            def attention(base, heads, maps, scale, bias=None):
                sc, tr, ou, _ = attention_groups(base, heads, maps)
                for s in range(heads + 2):
                    c = s % 2
                    if s < heads:
                        for j in range(maps):
                            g = sc[s, j]
                            full(dve, g)
                            src = bank[g % 8][:, :].rearrange("p (t k) -> p t k", t=NT)
                            if bias:
                                ap, factor = bias(s)
                                dve.scalar_tensor_tensor(sc_sb[:, c, j], ap, factor, src, ALU.mult,
                                                         ALU.add).then_inc(bank_moved[g % 8], 1)
                                moved(dve, g)
                                src = sc_sb[:, c, j]
                            link(dve.tensor_reduce(att[:, 0, c, j, :], src, AX, ALU.max))
                        dve.tensor_scalar(att[:, 1, c, 0:maps, :], att[:, 0, c, 0:maps, :], -scale, None,
                                          ALU.mult).then_inc(neg_max, 1)
                    if 1 <= s <= heads:
                        g = tr[s - 1]
                        full(dve, g)
                        dve.tensor_copy(pT[:, (s - 1) % 2].rearrange("p k q -> p (k q)"),
                                        bank[g % 8][:, :]).then_inc(bank_moved[g % 8], 1)
                    if s < heads:
                        if bias:
                            exps_done[0] += NT * maps
                            dve.wait_ge(exped, exps_done[0])
                        else:
                            moved(dve, sc[s, 0])
                        link(dve.reciprocal(att[:, 3, c, 0:maps, :], att[:, 2, c, 0:maps, :]))
                        if maps == 2:
                            link(dve.tensor_scalar(att[:, 3, c, 1, :], att[:, 3, c, 1, :], st[:, 14:15], None, ALU.mult))
                            for t in range(NT):
                                p1 = pr_sb[:, 2 * c + 1, t * S:t * S + S]
                                ins = dve.tensor_scalar(p1, p1, att[:, 3, c, 1, t:t + 1], None, ALU.mult)
                            link(ins)
                        for t in range(NT):
                            p0 = pr_sb[:, 2 * c, t * S:t * S + S]
                            r0 = att[:, 3, c, 0, t:t + 1]
                            if maps == 2:
                                ins = dve.scalar_tensor_tensor(p0, p0, r0, pr_sb[:, 2 * c + 1, t * S:t * S + S],
                                                               ALU.mult, ALU.add)
                            else:
                                ins = dve.tensor_scalar(p0, p0, r0, None, ALU.mult)
                        ins.then_inc(probs, 1)
                heads_done[0] += heads

            g = G["par"]
            full(dve, g)
            dve.tensor_copy(gainT[:, :], bank[g % 8][:, 0:G_END]).then_inc(bank_moved[g % 8], 1)
            for l in range(2):
                g = G["par"] + 1 + l
                full(dve, g)
                dve.tensor_copy(convT[:, l].rearrange("p a b c -> p (a b c)"),
                                bank[g % 8][:, 0:8 * FT]).then_inc(bank_moved[g % 8], 1)
            for g in range(G["par"], G["par"] + 3):
                moved(dve, g)
            dve.wait_ge(s_const, 16)

            x_transposed("x0", 0)
            g = G["mla_down"]
            dve.wait_ge(down_squares, 2)
            rsqrt(st[:, 20:22], st[:, 6:8], 2, 1.0 / QL)
            for t in range(NT):
                dve.tensor_scalar(cqn[:, t, :], bank[(g + t) % 8][:, 0:QL], st[:, 20 + t:21 + t], None,
                                  ALU.mult).then_inc(bank_moved[(g + t) % 8], 1)
            dve.wait_ge(down_squares, 4)
            rsqrt(st[:, 22:24], st[:, 8:10], 2, 1.0 / KVL)
            for t in range(NT):
                dve.tensor_scalar(ckvn[:, t, :], bank[(g + 2 + t) % 8][:, 0:KVL], st[:, 22 + t:23 + t], None, ALU.mult)
                rope(g + 2 + t, t, 1, krr[:, t, :].rearrange("p (a b) -> p a b", a=2), down_ready, off=KVL)
            for t in range(NT):
                g = G["mla_t"] + t
                full(dve, g)
                gained(g, cqT[:, :, t * P:t * P + P], blocks(bank[g % 8], 3), G_Q, 3)
            for t in range(NT):
                g = G["mla_t2"] + t
                full(dve, g)
                gained(g, ckvT[:, :, t * P:t * P + P], blocks(bank[g % 8], 2), G_KV, 2, moves=False)
                dve.tensor_copy(krT[:, t * P:t * P + P], bank[g % 8][:, 2 * P:3 * P]).then_inc(bank_moved[g % 8], 1)
            for t in range(NT):
                full(dve, G["mla_qr"] + t)
                rope(G["mla_qr"] + t, t, MH)
            attention(G["mla_att"], MH, 1, MLA_SCALE)
            full(dve, G["mla_o"] + 3)
            post(0, [(G["mla_o"] + n) % 8 for n in range(4)], range(G["mla_o"], G["mla_o"] + 4))

            def tile(n, b, par):
                x, u = [fbuf[b][a] for a in range(2)], [bank[b][:, a * S:a * S + S] for a in range(2)]
                dve.wait_ge(centre, 2 * n + 2)
                for a in range(2):
                    ins = dve.scalar_tensor_tensor(x[a][:, 1:S], u[a][:, 0:S - 1], par(0, a), x[a][:, 1:S],
                                                   ALU.mult, ALU.add)
                ins.then_inc(conv_step, 1)
                dve.wait_ge(conv_step, n + 1)
                for a in range(2):
                    ins = dve.scalar_tensor_tensor(x[a][:, 0:S - 1], u[a][:, 1:S], par(2, a), x[a][:, 0:S - 1],
                                                   ALU.mult, ALU.add)
                ins.then_inc(conv_done, 1)
                dve.wait_ge(g_squared, n + 1)
                dve.scalar_tensor_tensor(fbuf[b][3], fbuf[b][2], 1.0, x[0], ALU.add, ALU.mult).then_inc(g_inner, 1)
                dve.wait_ge(tanhed, n + 1)
                dve.scalar_tensor_tensor(fbuf[b][2], fbuf[b][5], 1.0, x[0], ALU.add, ALU.mult).then_inc(g_half, 1)
                dve.wait_ge(g_half, n + 1)
                dve.scalar_tensor_tensor(fbuf[b][4], fbuf[b][2], 0.5, x[1], ALU.mult, ALU.mult).then_inc(hid_ready, 1)

            def ffn(l):
                for j in range(4):
                    tile(l * FT + j, j % 3, lambda w, a: convT[:, l, w, a, j:j + 1])
                with dve.Fori(0, 3) as i:
                    dve.tensor_copy(cpar[:, :, :, :], convT[:, l, :, :, bass.ds(6 * i + 4, 6)]).then_inc(params_set, 1)
                    dve.wait_ge(params_set, i + (3 * l + 1))
                    for x in range(6):
                        tile(6 * i + (l * FT + 4 + x), (4 + x) % 3, lambda w, a: cpar[:, w, a, x:x + 1])

            x_transposed("x1", 1)
            ffn(0)
            dve.wait_ge(s_gains, 160)
            post(1, range(4, 8), None)

            x_transposed("x2", 2)
            lv = lamp[:, :, :].rearrange("p (a b) d -> p a b d", b=2)
            lp = scratch[:, 0:2 * HD].rearrange("p (a d) -> p a d", a=2)
            link(dve.tensor_tensor(lp, lv[:, :, 0, :], lv[:, :, 1, :], ALU.mult))
            dve.tensor_reduce(st[:, 10:12], lp, AX, ALU.add).then_inc(lam_dots, 1)
            dve.wait_ge(lam_exps, 1)
            link(dve.tensor_tensor(st[:, 14:15], st[:, 12:13], st[:, 13:14], ALU.subtract))
            link(dve.tensor_scalar(st[:, 14:15], st[:, 14:15], LAM_INIT, -1.0, ALU.add, ALU.mult))
            link(dve.tensor_scalar(st[:, 15:16], gainT[:, G_SUB:G_SUB + 1], 1.0 - LAM_INIT, None, ALU.mult))
            attention(G["diff_att"], DH, 2, HD_SCALE, lambda s: (dist, -(2.0 ** -(s + 1.0)) / HD_SCALE))
            for hd in range(DH):
                moved(dve, attention_groups(G["diff_att"], DH, 2)[2][hd])
            sq = r3(view(0, NT * D), b=D)
            for t in range(NT):
                ins = dve.tensor_tensor(sq[:, t], otok[:, t], otok[:, t], ALU.mult)
            link(ins)
            for t in range(NT):
                ins = dve.tensor_reduce(ss_o[:, 8 * t:8 * t + 8], sq[:, t].rearrange("p (h d) -> p h d", d=P), AX, ALU.add)
            link(ins)
            rsqrt(rs_o[:, 0:16], ss_o[:, 0:16], 16, 1.0 / P)
            for t in range(NT):
                o3 = otok[:, t].rearrange("p (h d) -> p h d", d=P)
                dve.tensor_tensor(o3, o3, spread(rs_o[:, 8 * t:8 * t + 8], 8, P), ALU.mult).then_inc(o_ready, 1)
            full(dve, G["diff_o"] + 3)
            post(2, [(G["diff_o"] + n) % 8 for n in range(4)], range(G["diff_o"], G["diff_o"] + 4))
            x_transposed("x3", 3)
            ffn(1)
            post(3, range(4, 8), None)

            x_transposed("x4", 4)
            for t in range(NT):
                full(dve, G["qi"] + t)
                rope(G["qi"] + t, t, 8)
            for t in range(NT):
                g = G["ki"] + t
                full(dve, g)
                full(dve, G["qi_t"] + t)
                dve.tensor_scalar(wi[:, t, :], bank[g % 8][:, HD:HD + 8], IDX_SCALE, None, ALU.mult)
                rope(g, t, 1, rr[:, t, 0:P].rearrange("p (a b) -> p a b", a=2), roped)
            for hd in range(8):
                moved(dve, G["index"] + hd)
                for t in range(NT):
                    r_ = relu[:, hd % 2, t * S:t * S + S]
                    if hd == 0:
                        ins = dve.tensor_scalar(score[:, t, :], r_, wi[:, t, 0:1], None, ALU.mult)
                    else:
                        ins = dve.scalar_tensor_tensor(score[:, t, :], r_, wi[:, t, hd:hd + 1], score[:, t, :],
                                                       ALU.mult, ALU.add)
                ins.then_inc(scored, 1)
                dve.wait_ge(scored, hd + 1)
            link(dve.tensor_tensor(score, score, caus, ALU.add))
            for r in range(TOPK // 8):
                for t in range(NT):
                    ins = dve.max(top8[:, t, :], work[r % 2][:, t, :])
                link(ins)
                for t in range(NT):
                    ins = dve.match_replace(work[1 - r % 2][:, t, :], top8[:, t, :], work[r % 2][:, t, :], -3e38)
                link(ins)
            link(dve.tensor_scalar(selm, work[0], -2e38, -NEG, ALU.is_le, ALU.mult))
            link(dve.scalar_tensor_tensor(selm, selm, NEG, caus, ALU.add, ALU.add))
            last_t = "ki_t"
            for a in "ab":
                for name in "qk":
                    for t in range(NT):
                        full(dve, G[name + a] + t)
                        full(dve, G[last_t] + t)
                        rope(G[name + a] + t, t, 8)
                    last_t = name + a + "_t"
            attention(G["moba_att"], 8, 1, HD_SCALE, lambda s: (caus, 1.0))
            attention(G["dsa_att"], 8, 1, HD_SCALE, lambda s: (selm, 1.0))
            for g in range(G["gates"], G["gates"] + 8):
                moved(dve, g)
            for t in range(NT):
                for hf in range(2):
                    g = G["pa"] + 2 * t + hf
                    full(dve, g)
                    x = siga[:, t, 512 * hf:512 * hf + 512]
                    dve.tensor_tensor(x, bank[g % 8][:, :], x, ALU.mult).then_inc(bank_moved[g % 8], 1)
            for t in range(NT):
                for hf in range(2):
                    g = G["pb"] + 2 * t + hf
                    full(dve, g)
                    dve.tensor_tensor(mtmp[:, 2 * t + hf, :], bank[g % 8][:, :], sigb[:, t, 512 * hf:512 * hf + 512],
                                      ALU.mult).then_inc(bank_moved[g % 8], 1)
            for g in range(G["pa"], G["pa"] + 8):
                moved(dve, g)
            for t in range(NT):
                dve.tensor_tensor(siga[:, t, :], siga[:, t, :],
                                  mtmp[:, 2 * t:2 * t + 2, :].rearrange("p a b -> p (a b)"), ALU.add).then_inc(mixed_ready, 1)
            for t in range(NT):
                for hf in range(2):
                    g = G["hyb_o"] + 2 * t + hf
                    full(dve, g)
                    x = h[:, t, 512 * hf:512 * hf + 512]
                    dve.tensor_tensor(x, x, bank[g % 8][:, :], ALU.add).then_inc(bank_moved[g % 8], 1)
                moved(dve, G["hyb_o"] + 2 * t + 1)
                dve.tensor_copy(st[:, 24:25], h[:, t, 0:1]).then_inc(h_ready, 1)

            x_transposed("x5", 5)
            for t in range(NT):
                g = G["router"] + t
                full(dve, g)
                dve.tensor_tensor(lg[:, t, :], bank[g % 8][:, 0:NG + NE], br[:, :], ALU.add).then_inc(bank_moved[g % 8], 1)
                moved(dve, g)
            link(dve.tensor_scalar(w8, cs[:, C_IOTA:C_IOTA + 8], -1.0, 8.0, ALU.mult, ALU.add))

            def minus_max(dst, src, top, n):
                link(dve.tensor_reduce(top, src, AX, ALU.max))
                return dve.tensor_tensor(dst, src, spread(top, NT, n), ALU.subtract)

            def first_max(hot, dif, top, n):
                w = w8[:, 0:n].unsqueeze(1).to_broadcast([P, NT, n])
                link(dve.scalar_tensor_tensor(hot, dif, 0.0, w, ALU.is_equal, ALU.mult))
                link(dve.tensor_reduce(top, hot, AX, ALU.max))
                link(dve.tensor_tensor(hot, hot, spread(top, NT, n), ALU.is_equal))

            minus_max(r_dif[0], lg[:, :, 0:NG], r_top[0], NG).then_inc(logits_max, 1)
            dve.wait_ge(logits_max, 1)
            first_max(r_hot[0], r_dif[0], r_top[1], NG)
            dve.wait_ge(logits_exp, 1)
            link(dve.tensor_reduce(r_top[2], r_exp[0], AX, ALU.add))
            link(dve.reciprocal(r_top[2], r_top[2]))
            for t in range(NT):
                ins = dve.tensor_tensor(r_prod[:, t], lg[:, t, NG:].rearrange("p (g e) -> p g e", g=NG),
                                        r_hot[0][:, t, :].unsqueeze(2).to_broadcast([P, NG, EPG]), ALU.mult)
            link(ins)
            link(dve.tensor_reduce(r_sel, r_prod.rearrange("p t g e -> p t e g"), AX, ALU.add))
            minus_max(r_dif[1], r_sel, r_top[0], EPG).then_inc(logits_max, 1)
            dve.wait_ge(logits_exp, 2)
            for n in range(2):
                link(minus_max(r_dif[1], r_exp[1], r_top[3 + n], EPG))
                first_max(r_hot[1 + n], r_dif[1], r_top[0], EPG)
                if n == 0:
                    link(dve.scalar_tensor_tensor(r_exp[1], r_hot[1], -4.0, r_exp[1], ALU.mult, ALU.add))
            link(dve.tensor_tensor(r_top[0], r_top[3], r_top[4], ALU.add))
            link(dve.reciprocal(r_top[0], r_top[0]))
            link(dve.tensor_tensor(r_top[0], r_top[0], r_top[2], ALU.mult))
            for n in range(2):
                link(dve.tensor_tensor(r_top[3 + n], r_top[3 + n], r_top[0], ALU.mult))
                link(dve.tensor_tensor((r_sel, r_dif[1])[n], r_hot[1 + n], spread(r_top[3 + n], NT, EPG), ALU.mult))
            link(dve.tensor_tensor(r_sel, r_sel, r_dif[1], ALU.add))
            link(dve.tensor_tensor(r_hot[1], r_hot[1], r_hot[2], ALU.add))
            for dst, src in [(gate, r_sel), (mask, r_hot[1])]:
                for t in range(NT):
                    ins = dve.tensor_tensor(dst[:, t].rearrange("p (g e) -> p g e", g=NG),
                                            r_hot[0][:, t, :].unsqueeze(2).to_broadcast([P, NG, EPG]),
                                            src[:, t, :].unsqueeze(1).to_broadcast([P, NG, EPG]), ALU.mult)
            ins.then_inc(mask_ready, 1)
            dve.wait_ge(mask_ready, 1)
            g = G["pos"]
            full(dve, g)
            link(dve.scalar_tensor_tensor(posm, bank[g % 8][:, 0:2 * NE].rearrange("p (t e) -> p t e", t=NT), 1.0, mask,
                                          ALU.add, ALU.mult))
            link(dve.tensor_scalar(posm, posm, -1.0, None, ALU.add))
            dve.tensor_reduce(st[:, 25:26], bank[g % 8][:, 2 * NE:3 * NE], AX, ALU.max).then_inc(bank_moved[g % 8], 1)
            moved(dve, g)
            dve.tensor_scalar(flag[:, :], st[:, 25:26], CAP + 0.5, None, ALU.is_gt).then_inc(flag_ready, 1)

            iota = cs[:, C_IOTA:C_IOTA + CAP].unsqueeze(1).to_broadcast([P, 2, CAP])

            def of_pair(ap, t, i):
                return ap[:, t, bass.ds(2 * i, 2)].unsqueeze(2).to_broadcast([P, 2, CAP])

            def select(n, i):
                for t in range(NT):
                    ins = dve.tensor_tensor(Sel[:, t], iota, of_pair(posm, t, i), ALU.is_equal)
                ins.then_inc(sel_ready, 1)

            def take(n):
                dve.wait_ge(xg_full, 1 + n)
                for q in range(2):
                    dve.tensor_tensor(XgT[:, 4 * q:4 * q + 4, :], blocks(bank[2 + q], 4),
                                      spread(gainT[:, G_N[5] + 4 * q:G_N[5] + 4 * q + 4], 4, P), ALU.mult).then_inc(xg_ready, 1)

            def pair(n, i, last=False):
                dve.wait_ge(sel_ready, 1 + n)
                for t in range(NT):
                    ins = dve.tensor_tensor(SelG[:, t], Sel[:, t], of_pair(gate, t, i), ALU.mult)
                ins.then_inc(selg_ready, 1)
                if not last:
                    dve.wait_ge(selg_ready, 1 + n)
                    select(n + 1, i + 1)
                dve.wait_ge(h3_full, 1 + n)
                dve.wait_ge(silu_ready, 1 + n)
                dve.tensor_tensor(hid, silu, bank[1][:, :], ALU.mult).then_inc(hidden_ready, 1)
                if not last:
                    take(n + 1)
                dve.wait_ge(sgT_full, 1 + n)
                dve.tensor_copy(SgT.rearrange("p a b -> p (a b)"), bank[0][:, 0:NT * P]).then_inc(sgT_ready, 1)

            def one_round(base):
                select(base, 0)
                take(base)
                with dve.Fori(0, NP - 1) as i:
                    pair(base + i, i)
                pair(base + (NP - 1), NP - 1, last=True)

            one_round(0)
            over = dve.value_load(flag[0:1, 0:1], min_val=0, max_val=1)
            with dve.If(over):
                with dve.Fori(1, ROUNDS) as r:
                    dve.tensor_scalar(posm, posm, -float(CAP), None, ALU.add).then_inc(pos_step, 1)
                    dve.wait_ge(pos_step, r)
                    one_round(r * NP)

            dve.wait_ge(moe_full, 1)
            for t in range(NT):
                for hf in range(2):
                    x = h[:, t, 512 * hf:512 * hf + 512]
                    ins = dve.tensor_tensor(x, x, bank[4 + 2 * t + hf][:, :], ALU.add)
                ins.then_inc(h_ready, 1)
            dve.wait_ge(h_squares, 14)
            rsqrt(st[:, 16:18], st[:, 0:2], 2, 1.0 / D)
            for t in range(NT):
                dve.scalar_tensor_tensor(xn[:, t, :], h[:, t, :], st[:, 16 + t:17 + t], gpost[:, 4, :],
                                         ALU.mult, ALU.mult).then_inc(out_ready, 1)


_INS = ["x", "norm_g", "ffn_w_up", "ffn_conv_w", "ffn_conv_b", "ffn_w_down", "mla_w_dq", "mla_q_norm_g", "mla_w_uq",
        "mla_w_dkv", "mla_kv_norm_g", "mla_w_ukv", "mla_w_o", "diff_w_qkv", "diff_lambda", "diff_subln_g", "diff_w_o",
        "g_mix_2", "w_in_2", "w_proj_a_2", "w_proj_b_2", "w_out_2", "g_ffn_2", "w_group_2", "b_group_2", "w_expert_2",
        "b_expert_2", "w1_2", "w3_2", "w2_2", "g_final_2"]


def kernel(**inputs):
    import concourse.bacc as _bacc
    from concourse.bass_utils import run_bass_kernel_spmd as _run

    nc = _bacc.Bacc("TRN2", target_bir_lowering=False, num_devices=1)
    arrays, aps = {}, {}
    for name in _INS:
        a = np.ascontiguousarray(inputs[name])
        arrays[f"in_{name}"] = a
        aps[name] = nc.dram_tensor(f"in_{name}", a.shape, mybir.dt.from_np(a.dtype), kind="ExternalInput").ap()
    arrays["constants"] = constants()
    cst = nc.dram_tensor("constants", (P, C_END), F32, kind="ExternalInput").ap()
    out = nc.dram_tensor("out", (1, S, D), F32, kind="ExternalOutput").ap()
    build(nc, aps, cst, out)
    r = _run(nc, [arrays], core_ids=[0])
    return r.results[0]["out"]
```

```python
from contextlib import ExitStack

import numpy as np

import concourse.bass as bass
from concourse import mybir

F32 = mybir.dt.float32
F32R = mybir.dt.float32r
I32 = mybir.dt.int32
ALU = mybir.AluOpType
ACT = mybir.ActivationFunctionType
AX = mybir.AxisListType.X

P = 128
S = 256
NT = S // P
D = 1024
KT = D // P
EPS = 1e-6
NEG = -1e30

QL, KVL = 384, 256
MH, MN, MR = 8, 128, 64
MLA_SCALE = float(MN + MR) ** -0.5
DH = 8
HD = 64
HD_SCALE = float(HD) ** -0.5
F = 2816
FT = F // P
FM = FT // 2
LAM_INIT = 0.8 - 0.6 * float(np.exp(-0.3))
TOPK = min(256, S // 4)
IDX_SCALE = float(8 * 64) ** -0.5
NE, EF = 32, 512
NG, EPG = 4, 8
CAP = 64
ROUNDS = S // CAP
NP = NE // 2

PIECE = 2048
RING = 6
PARTS = 3
SLOT = 4096
SLOTS = 6

C_ID, C_TRI, C_ONE, C_IOTA = 0, 128, 256, 384
C_DIST = 448
C_CAUS = C_DIST + NT * S
C_COS = C_CAUS + NT * S
C_SIN = C_COS + NT * HD
C_END = C_SIN + NT * HD

def constants():
    c = np.zeros((P, C_END), np.float32)
    i = np.arange(P)
    c[:, C_ID:C_ID + P] = np.eye(P)
    c[:, C_TRI:C_TRI + P] = i[:, None] < i[None, :]
    c[:, C_ONE:C_ONE + P] = 1.0
    c[:, C_IOTA:C_IOTA + CAP] = np.arange(CAP)[None]
    k = np.arange(S)
    inv = np.float32(10000.0) ** (-np.arange(0, HD, 2, dtype=np.float32) / np.float32(HD))
    for t in range(NT):
        q = i + t * P
        c[:, C_DIST + t * S:C_DIST + (t + 1) * S] = np.abs(q[:, None] - k[None, :])
        c[:, C_CAUS + t * S:C_CAUS + (t + 1) * S] = np.where(k[None, :] <= q[:, None], 0.0, NEG)
        ang = q.astype(np.float32)[:, None] * inv[None, :]
        c[:, C_COS + t * HD:C_COS + (t + 1) * HD] = np.tile(np.cos(ang), 2)
        c[:, C_SIN + t * HD:C_SIN + t * HD + 32] = -np.sin(ang)
        c[:, C_SIN + t * HD + 32:C_SIN + (t + 1) * HD] = np.sin(ang)
    return c


STAGES = {"mla_att": (MH, 1, 0), "diff_att": (DH, 2, 4), "moba_att": (8, 1, 4), "dsa_att": (8, 1, 4)}


def attention_groups(name, base):
    heads, maps, between = STAGES[name]
    sc, tr, ou, g = {}, {}, {}, base
    for s in range(heads + 3):
        if s < heads:
            for j in range(maps):
                sc[s, j] = g
                g += 1
        if s == 1:
            g += between
        if 2 <= s < heads + 2:
            tr[s - 2] = g
            g += 1
        if s >= 3:
            ou[s - 3] = g
            g += 1
    return sc, tr, ou, g - base


def plan():
    G, g = {}, 0
    for name, n in [
        ("x0", 4), ("mla_down", 4), ("mla_t", 2), ("mla_t2", 2), ("mla_qn", 4), ("mla_qr", 2),
        ("mla_kv", 8), ("mla_qrt", 2), ("mla_att", attention_groups("mla_att", 0)[3]), ("par", 3), ("mla_o", 4),
        ("x1", 4), ("x2", 4),
        ("diff_q", 8), ("diff_att", attention_groups("diff_att", 0)[3]),
        ("diff_t", 4), ("diff_o", 4), ("x3", 4), ("x4", 4),
        ("qi", 2), ("ki", 2), ("qi_t", 2), ("qa", 2), ("ki_t", 2), ("index", 8),
        ("ka", 2), ("qa_t", 2), ("va", 2), ("ka_t", 2),
        ("qb", 2), ("kb", 2), ("qb_t", 2), ("vb", 2), ("kb_t", 2),
        ("moba_att", attention_groups("moba_att", 0)[3]),
        ("gb", 4), ("dsa_att", attention_groups("dsa_att", 0)[3]), ("pb", 4),
        ("mix_t", 4), ("hyb_o", 4), ("x5", 4), ("router", 2), ("pos", 1),
    ]:
        G[name] = g
        g += n
    G["diff_v"], G["ga"], G["pa"] = G["diff_att"] + 4, G["moba_att"] + 2, G["dsa_att"] + 2
    W, w = {}, 0
    for name, n in [
        ("dq", 2), ("dkv", 2), ("uq", 4), ("ukv", 2), ("mla_wo", 4), ("ffn0", 3 * FM),
        ("qk", 8), ("v", 4), ("diff_wo", 4), ("ffn1", 3 * FM),
        ("qi", 2), ("ki", 1), ("qa", 2), ("ka", 2), ("va", 2), ("qb", 2), ("kb", 2), ("vb", 2),
        ("ga", 4), ("gb", 4), ("pa", 2), ("pb", 2), ("wout", 4), ("end", 0),
    ]:
        W[name] = w
        w += n
    return G, W


def build(nc, A, cst, out):
    G, W = plan()
    ctx = ExitStack()
    with ctx:
        def sb(name, shape, dt=F32):
            return ctx.enter_context(nc.sbuf_tensor(name, shape, dt))

        def sem(name):
            return ctx.enter_context(nc.semaphore(name))

        bank = [ctx.enter_context(nc.psum_tensor(f"bank{b}", [P, 512], F32)) for b in range(8)]
        with nc.sbuf_tensor("raw", [P, RING, PIECE], F32) as raw, \
                nc.sbuf_tensor("high", [P, PARTS, PIECE], F32R) as high, \
                nc.sbuf_tensor("low", [P, PARTS, PIECE], F32R) as low:
            pass
        ring = sb("ring", [P, SLOTS, SLOT])
        cs = sb("cs", [P, C_END])
        prow = sb("prow", [P, 5, P])
        subT = sb("subT", [P, 1])
        convT = sb("convT", [P, 2, 4, 2, FT])
        gpre, gpost = sb("gpre", [P, D]), sb("gpost", [P, D])
        wr = sb("wr", [P, KT, NG + NE])
        br = sb("br", [P, NG + NE])
        lamp = sb("lamp", [P, 4, HD])
        h = sb("h", [P, NT, D])
        xn = sb("xn", [P, NT, D])
        xh, xl = sb("xh", [P, KT, S], F32R), sb("xl", [P, KT, S], F32R)
        hh, hl = sb("hh", [P, 4, S], F32R), sb("hl", [P, 4, S], F32R)
        st = sb("st", [P, 64])
        eps_t = sb("eps_t", [P, 8])
        att = sb("att", [P, 4, 2, 2, 2])
        room = sb("room", [P, 11648])

        def view(at, n):
            return room[:, at:at + n]

        def r3(ap, **k):
            return ap.rearrange("p (a b) -> p a b", **k)

        qT, kT = r3(view(0, 2048), b=S), r3(view(2048, 2048), b=S)
        vtok = r3(view(4096, 2048), b=D)
        otok = r3(view(6144, 2048), b=D)
        sc_sb = view(8192, 2048).rearrange("p (c j t k) -> p c j t k", c=2, j=2, t=NT)
        rt = r3(view(8192, 1024), b=512)
        qrT = r3(view(9216, 1024), b=S)
        rr = r3(view(10240, 1024), b=512)
        pT = view(10240, 1024).rearrange("p (c k q) -> p c k q", c=2, k=NT)
        krT = view(11264, 256)
        scratch = view(11520, 128)
        pr_sb = xn[:, :, :].rearrange("p a (b c) -> p (a b) c", c=NT * S)

        def prob(hd, j, maps, t, k0=0, n=S):
            return pr_sb[:, (maps * hd + j) % 4, t * S + k0:t * S + k0 + n]

        cqn, ckvn = r3(view(0, 2 * QL), b=QL), r3(view(2048, NT * KVL), b=KVL)
        krr = r3(view(4096, NT * P), b=P)
        cq, ckv = (xh[:, 0:3], xl[:, 0:3]), (xh[:, 3:5], xl[:, 3:5])
        qaT, kaT = r3(view(0, 1024), b=S), r3(view(1024, 1024), b=S)
        qbT, kbT = r3(view(2048, 1024), b=S), r3(view(3072, 1024), b=S)
        va, vb = r3(view(4096, 1024), b=512), r3(view(5120, 1024), b=512)
        qiT, kiT = qrT, krT
        relu = r3(view(6144, 1024), b=NT * S)
        score = sb("score", [P, NT, S])
        selm = r3(prow[:, 0:4, :].rearrange("p a b -> p (a b)"), b=S)
        work = [score[:, :, :], selm]
        siga, sigb = r3(view(6144, 2048), b=D), r3(view(0, 2048), b=D)
        mtmp = r3(view(2048, 2048), b=512)
        fbuf = [[view((6 * b + x) * S, S) for x in range(6)] for b in range(4)]
        cpar = view(24 * S, 32).rearrange("p (a b c) -> p a b c", a=4, b=2)
        XgT = r3(view(0, KT * P), b=P)
        hid = view(1024, EF)
        silu = view(1536, EF)
        hidT = r3(view(2048, EF), b=P)
        ysb = view(2560, D)
        Sel = view(3584, NT * 2 * CAP).rearrange("p (t e c) -> p t e c", t=NT, e=2)
        SelG = view(3840, NT * 2 * CAP).rearrange("p (t e c) -> p t e c", t=NT, e=2)
        SgT = r3(view(4096, NT * P), b=P)
        gate, posm, mask = (r3(view(4352 + 64 * n, NT * NE), b=NE) for n in range(3))
        lg = r3(view(4608, NT * 36), b=36)
        rb = view(4700, 512)
        xT = r3(view(8192, 2048), b=S)
        flag = sb("flag", [P, 1], I32)
        wi, top8 = sb("wi", [P, NT, 8]), sb("top8", [P, NT, 8])
        ss_o, rs_o = sb("ss_o", [P, 16]), sb("rs_o", [P, 16])
        w8 = rb[:, 0:8]
        r_top = [rb[:, 8 + 2 * n:10 + 2 * n] for n in range(5)]
        r_dif = [r3(rb[:, 24:32], b=NG), r3(rb[:, 32:48], b=EPG)]
        r_exp = [r3(rb[:, 48:56], b=NG), r3(rb[:, 56:72], b=EPG)]
        r_hot = [r3(rb[:, 72:80], b=NG), r3(rb[:, 80:96], b=EPG), r3(rb[:, 96:112], b=EPG)]
        r_sel = r3(rb[:, 112:128], b=EPG)
        r_prod = rb[:, 128:192].rearrange("p (t g e) -> p t g e", t=NT, g=NG)

        bank_full = [sem(f"bank_full{b}") for b in range(8)]
        bank_moved = [sem(f"bank_moved{b}") for b in range(8)]
        arrived = [[sem(f"arrived{c}_{a}") for a in range(2)] for c in range(SLOTS)]
        halves_used = sem("halves_used")
        piece_here = [sem(f"piece_here{b}") for b in range(RING)]
        high_ready, low_ready, pieces_used = sem("high_ready"), sem("low_ready"), sem("pieces_used")
        x_high = sem("x_high")
        gpre_here, gpost_here = sem("gpre_here"), sem("gpost_here")
        s_const, s_tables, s_rows, s_x, s_gains, s_mla = (
            sem(n) for n in ("s_const", "s_tables", "s_rows", "s_x", "s_gains", "s_mla"))
        vec = sem("vec")
        h_ready, h_squares = sem("h_ready"), sem("h_squares")
        eps_set, sums_ready, guessed = sem("eps_set"), sem("sums_ready"), sem("guessed")
        xn_ready = sem("xn_ready")
        down_squares, down_ready = sem("down_squares"), sem("down_ready")
        roped = sem("roped")
        post_squares = sem("post_squares")
        neg_max, exped, probs = sem("neg_max"), sem("exped"), sem("probs")
        o_ready, scored, mixed_ready = sem("o_ready"), sem("scored"), sem("mixed_ready")
        lam_dots, lam_exps = sem("lam_dots"), sem("lam_exps")
        up_full, centre, conv_done = sem("up_full"), sem("centre"), sem("conv_done")
        conv_step, g_squared, g_inner, tanhed, g_half, hid_high, hid_ready = (
            sem(n) for n in ("conv_step", "g_squared", "g_inner", "tanhed", "g_half", "hid_high", "hid_ready"))
        params_set, ffn_full = sem("params_set"), sem("ffn_full")
        logits_max, logits_exp, mask_ready, flag_ready = (
            sem(n) for n in ("logits_max", "logits_exp", "mask_ready", "flag_ready"))
        sel_ready, selg_ready, xg_full, xg_ready, h1_full, h3_full, silu_ready, hidden_ready = (
            sem(n) for n in ("sel_ready", "selg_ready", "xg_full", "xg_ready", "h1_full", "h3_full",
                             "silu_ready", "hidden_ready"))
        hidT_full, hidT_ready, sgT_full, sgT_ready, y_full, y_ready, pos_step, moe_full = (
            sem(n) for n in ("hidT_full", "hidT_ready", "sgT_full", "sgT_ready", "y_full", "y_ready",
                             "pos_step", "moe_full"))
        zeros_ready = sem("zeros_ready")
        out_ready, stored = sem("out_ready"), sem("stored")

        def full(eng, g):
            eng.wait_ge(bank_full[g % 8], g // 8 + 1)

        def moved(eng, g):
            eng.wait_ge(bank_moved[g % 8], g // 8 + 1)

        def slot(c, k, n):
            return ring[:, c, 0:k * n].rearrange("p (k n) -> p k n", k=k)

        def parts(p, k, n):
            return [x[:, p % PARTS, 0:k * n].rearrange("p (k n) -> p k n", k=k) for x in (high, low)]

        def have(eng, c, a, turn):
            for e in range(2):
                eng.wait_ge(arrived[c + e][a], 16 * turn + 16)

        ident = cs[:, C_ID:C_ID + P]
        caus = r3(cs[:, C_CAUS:C_CAUS + NT * S], b=S)
        dist = r3(cs[:, C_DIST:C_DIST + NT * S], b=S)
        cos = r3(cs[:, C_COS:C_COS + NT * HD], b=HD)
        sin = r3(cs[:, C_SIN:C_SIN + NT * HD], b=HD)

        WIDTH = [PIECE] * W["end"]
        for name, widths in [("dq", [5 * QL, 3 * QL]), ("dkv", [6 * (KVL + MR), 2 * (KVL + MR)]),
                             ("uq", [3 * 384] * 4), ("ki", [8 * 72])]:
            WIDTH[W[name]:W[name] + len(widths)] = widths

        TILES = [(t, 0) for t in range(NT)]
        TILE_HALVES = [(t, q) for t in range(NT) for q in range(2)]
        HALVES = [(t, q) for q in range(2) for t in range(NT)]

        block = ctx.enter_context(nc.Block())

        @block.sync
        def _(sp):
            def load(p, moves, turn=0):
                if p >= RING:
                    sp.wait_ge(low_ready, p - RING + 1 + RING * turn)
                for dst, src in moves:
                    sp.dma_start(dst, src).then_inc(piece_here[p % RING], 16)

            def weights(p, w, pieces):
                w = w.rearrange("(k p) n -> p k n", p=P)
                for k0, k, c0, n in pieces:
                    d = raw[:, p % RING, 0:k * n].rearrange("p (k n) -> p k n", k=k)
                    s = w[:, k0:k0 + k, c0:c0 + n]
                    a = k // 2
                    load(p, [(d[:, :a], s[:, :a]), (d[:, a:], s[:, a:])])
                    p += 1

            def rows_on(dst, src):
                sp.dma_start(dst, src.rearrange("(r m) -> r m", m=P)).then_inc(s_rows, 16)

            def pre_gains(n, src):
                if n:
                    sp.wait_ge(xn_ready, 4 * n)
                sp.dma_start(gpre[:, :], src.partition_broadcast(P)).then_inc(gpre_here, 16)

            def post_gains(n, src):
                sp.wait_ge(*((h_ready, 2 * n) if n else (down_ready, 2)))
                sp.dma_start(gpost[:, :], src.partition_broadcast(P)).then_inc(gpost_here, 16)

            for t in range(NT):
                sp.dma_start(h[:, t, :], A["x"][0, t * P:t * P + P, :]).then_inc(s_x, 16)
            sp.dma_start(cs[:, C_ID:C_ID + P], cst[:, C_ID:C_ID + P]).then_inc(s_const, 16)
            weights(W["dq"], A["mla_w_dq"][0], [(0, 5, 0, QL)])
            pre_gains(0, A["norm_g"][0, 0])
            weights(W["dq"] + 1, A["mla_w_dq"][0], [(5, 3, 0, QL)])
            two = [(0, 4, 0, 512), (4, 4, 0, 512)]
            weights(W["dkv"], A["mla_w_dkv"][0], [(0, 6, 0, KVL + MR), (6, 2, 0, KVL + MR)])
            sp.dma_start(cs[:, P:], cst[:, P:]).then_inc(s_tables, 16)
            sp.dma_start(gpost[:, 0:QL], A["mla_q_norm_g"][0].partition_broadcast(P)).then_inc(s_mla, 16)
            sp.dma_start(gpost[:, QL:QL + KVL], A["mla_kv_norm_g"][0].partition_broadcast(P)).then_inc(s_mla, 16)
            weights(W["uq"], A["mla_w_uq"][0], [(0, 3, 384 * n, 384) for n in range(4)])
            for l in range(2):
                for w in range(2):
                    rows_on(prow[44 * w:44 * w + 44, 2 * l, :], A["ffn_conv_w"][l, w])
                rows_on(prow[0:44, 1 + 2 * l, :], A["ffn_conv_w"][l, 2])
                rows_on(prow[44:88, 1 + 2 * l, :], A["ffn_conv_b"][l])
            rows_on(prow[0:1, 4, :], A["diff_subln_g"][0])
            weights(W["ukv"], A["mla_w_ukv"][0], [(0, 2, 1024 * n, 1024) for n in range(2)])
            pre_gains(1, A["norm_g"][0, 2])
            post_gains(0, A["norm_g"][0, 1])
            sp.dma_start(lamp[:, :, :].rearrange("p a b -> p (a b)"),
                         A["diff_lambda"][0].rearrange("a b -> (a b)").partition_broadcast(P)).then_inc(s_gains, 16)
            sp.dma_start(br[:, 0:NG], A["b_group_2"][0].partition_broadcast(P)).then_inc(s_gains, 16)
            sp.dma_start(br[:, NG:], A["b_expert_2"][0].partition_broadcast(P)).then_inc(s_gains, 16)
            sp.dma_start(wr[:, :, 0:NG], A["w_group_2"][0].rearrange("(k p) n -> p k n", p=P)).then_inc(s_gains, 16)
            sp.dma_start(wr[:, :, NG:], A["w_expert_2"][0].rearrange("(k p) n -> p k n", p=P)).then_inc(s_gains, 16)

            def square(p, w):
                weights(p, w, [(k, 2, 0, D) for k in range(0, w.shape[0] // P, 2)])

            def ffn_up(p, l, j, turn=0):
                w = A["ffn_w_up"][l].rearrange("(k p) (a n) -> p k a n", p=P, a=2)
                d = raw[:, p % RING, :].rearrange("p (k a n) -> p k a n", a=2, n=P)
                load(p, [(d[:, :, a], w[:, :, a, bass.ds(j * P, P)]) for a in range(2)], turn)

            def ffn_down(p, l, m, turn=0):
                w = A["ffn_w_down"][l].rearrange("(k p) n -> p k n", p=P)
                d = raw[:, p % RING, :].rearrange("p (k n) -> p k n", n=D)
                load(p, [(d[:, x:x + 1], w[:, bass.ds(2 * m + x, 1)]) for x in range(2)], turn)

            def ffn(l, behind):
                b = W[f"ffn{l}"]
                ffn_up(b, l, 0)
                ffn_up(b + 1, l, 1)
                for m in range(1, 3):
                    ffn_up(b + 3 * m - 1, l, 2 * m)
                    ffn_up(b + 3 * m, l, 2 * m + 1)
                    ffn_down(b + 3 * m + 1, l, m - 1)
                behind()
                with sp.Fori(0, 4) as i:
                    for s in range(2):
                        ffn_up(b + 8 + 3 * s, l, 4 * i + (6 + 2 * s), i)
                        ffn_up(b + 9 + 3 * s, l, 4 * i + (7 + 2 * s), i)
                        ffn_down(b + 10 + 3 * s, l, 2 * i + (2 + s), i)
                ffn_down(b + 32, l, 10)

            square(W["mla_wo"], A["mla_w_o"][0])

            def behind0():
                pre_gains(2, A["norm_g"][1, 0])
                post_gains(1, A["norm_g"][0, 3])

            ffn(0, behind0)
            weights(W["qk"], A["diff_w_qkv"][0], [(0, 8, 256 * n, 256) for n in range(8)])
            pre_gains(3, A["norm_g"][1, 2])
            post_gains(2, A["norm_g"][1, 1])
            for n in range(2):
                weights(W["v"] + 2 * n, A["diff_w_qkv"][0][:, 2048 + 512 * n:2560 + 512 * n], two)
            square(W["diff_wo"], A["diff_w_o"][0])

            def behind1():
                pre_gains(4, A["g_mix_2"][0])
                post_gains(3, A["norm_g"][1, 3])

            ffn(1, behind1)
            w_in = A["w_in_2"][0]
            for name, at in [("qi", 3072), ("ki", 3584), ("qa", 0), ("ka", 512), ("va", 1024), ("qb", 1536),
                             ("kb", 2048), ("vb", 2560)]:
                if name == "ki":
                    weights(W[name], w_in[:, at:at + 72], [(0, 8, 0, 72)])
                else:
                    weights(W[name], w_in[:, at:at + 512], two)
                if name == "vb":
                    pre_gains(5, A["g_ffn_2"][0])
                    post_gains(4, A["g_final_2"])
            for x, at in [("a", 3656), ("b", 4680)]:
                for n in range(2):
                    weights(W["g" + x] + 2 * n, w_in[:, at + 512 * n:at + 512 * n + 512], two)
            for x in "ab":
                square(W["p" + x], A[f"w_proj_{x}_2"][0])
            square(W["wout"], A["w_out_2"][0])

            def pair(i, turn, first=False):
                for x, (name, k, n) in enumerate([("w1_2", KT, EF), ("w3_2", KT, EF), ("w2_2", 4, D)]):
                    w = A[name][0].rearrange("e (k p) n -> p e k n", p=P)
                    for a in range(2):
                        for e in range(2):
                            c = 2 * x + e
                            if not first:
                                if e == 0:
                                    sp.wait_ge(halves_used, 4 * x + 2 * a + 2 + (turn - 1) * 2 * SLOTS)
                            elif c == 0 and a == 0:
                                sp.wait_ge(low_ready, W["end"])
                            elif c == 3 and a == 0:
                                sp.wait_ge(pieces_used, W["end"])
                            sp.dma_start(slot(c, k, n)[:, a * k // 2:(a + 1) * k // 2],
                                         w[:, bass.ds(2 * i + e, 1), a * k // 2:(a + 1) * k // 2, :].rearrange(
                                             "p e k n -> p (e k) n")).then_inc(arrived[c][a], 16)

            pair(0, 0, first=True)
            with sp.Fori(1, NP) as i:
                pair(i, i)
            sp.wait_ge(flag_ready, 1)
            over = sp.value_load(flag[0:1, 0:1], min_val=0, max_val=1)
            with sp.If(over):
                with sp.Fori(1, ROUNDS) as r:
                    with sp.Fori(0, NP) as i:
                        pair(i, r * NP + i)
            for t in range(NT):
                sp.wait_ge(out_ready, t + 1)
                sp.dma_start(out[0, t * P:t * P + P, :], xn[:, t, :]).then_inc(stored, 16)
            sp.wait_ge(stored, 16 * NT)

        @block.gpsimd
        def _(pool):
            def lows(p, n=PIECE, turn=0):
                pool.wait_ge(high_ready, p + 1 + RING * turn)
                pool.tensor_tensor(low[:, p % PARTS, 0:n], raw[:, p % RING, 0:n], high[:, p % PARTS, 0:n],
                                   ALU.subtract).then_inc(low_ready, 1)

            p = 0
            for l in range(2):
                while p < W[f"ffn{l}"] + 8:
                    lows(p, WIDTH[p])
                    p += 1
                with pool.Fori(0, 4) as i:
                    for x in range(RING):
                        lows(p + x, turn=i)
                p += 4 * RING
            while p < W["end"]:
                lows(p, WIDTH[p])
                p += 1

        @block.tensor
        def _(pe):
            owed = [0]

            def behind(ins):
                if owed[0]:
                    ins.then_inc(pieces_used, owed[0])
                owed[0] = 0

            def begin(g):
                if g >= 8:
                    moved(pe, g - 8)
                return bank[g % 8]

            def end(ins, g):
                ins.then_inc(bank_full[g % 8], 1)

            def product(out_, a, b, start, stop):
                first = pe.matmul(out_, a[0], b[0], start=start, stop=False)
                pe.matmul(out_, a[0], b[1], start=False, stop=False)
                return first, pe.matmul(out_, a[1], b[0], start=False, stop=stop)

            def transposes(g, blocks):
                b = begin(g)
                at = 0
                for n, src in enumerate(blocks):
                    rows, cols = src.shape[0], src.shape[1]
                    ins = pe.transpose(b[0:cols, at:at + rows], src, ident[0:rows, 0:rows])
                    if n == 0 and len(blocks) > 1:
                        behind(ins)
                    at += rows
                end(ins, g)

            def x_transposed(name, site):
                for q in range(2):
                    for t in range(NT):
                        pe.wait_ge(xn_ready, 4 * site + 2 * q + t + 1)
                        transposes(G[name] + 2 * q + t, [xn[:, t, P * k:P * k + P] for k in range(4 * q, 4 * q + 4)])
                for t in range(NT):
                    moved(pe, G[name] + t)
                late.extend([G[name] + 2, G[name] + 3])

            def keep_clock(n, b):
                for _ in range(n):
                    pe.matmul(b[:, :], xh[:, 0, 0:P], xh[:, 0:2, :], start=True, stop=True)

            WAIT = 32
            late = []

            def k_tile(k):
                if k == 4:
                    while late:
                        moved(pe, late.pop(0))

            def by_token(g0, p0, x, k_counts, widths, order=None):
                cols = [(c, t) for c in range(len(widths)) for t in range(NT)]
                group = {ct: g0 + (order(*ct) if order else n) for n, ct in enumerate(cols)}
                for ct in sorted(cols, key=lambda ct: group[ct]):
                    begin(group[ct])
                k0 = 0
                for n, ks in enumerate(k_counts):
                    p = p0 + n
                    pe.wait_ge(low_ready, p + 1)
                    w = parts(p, ks, sum(widths))
                    for ct in sorted(cols, key=lambda ct: group[ct]):
                        c, t = ct
                        at = sum(widths[:c])
                        for k in range(ks):
                            k_tile(k0 + k)
                            first, ins = product(bank[group[ct] % 8][:, 0:widths[c]],
                                                 [y[:, k0 + k, t * P:t * P + P] for y in x],
                                                 [y[:, k, at:at + widths[c]] for y in w],
                                                 k0 + k == 0, n == len(k_counts) - 1 and k == ks - 1)
                            behind(first)
                        if n == len(k_counts) - 1:
                            end(ins, group[ct])
                    owed[0] += 1
                    k0 += ks

            def by_feature(g, ws, x, kt):
                b = begin(g)
                for n, w in enumerate(ws):
                    for k in range(kt):
                        k_tile(k)
                        first, ins = product(b[:, n * S:n * S + S], [y[:, k] for y in w], [y[:, k, :] for y in x],
                                             k == 0, k == kt - 1)
                        behind(first)
                end(ins, g)

            def square_out(name, p0, x):
                by_token(G[name], p0, x, [2] * (x[0].shape[1] // 2), [512, 512], order=lambda c, t: 2 * t + c)

            def attention(name, q_of, k_of, values, by_tokens, ready, between=None):
                heads, maps, _ = STAGES[name]
                sc, tr, ou, _ = attention_groups(name, G[name])
                for g in ready:
                    moved(pe, g)
                for s in range(heads + 3):
                    if s < heads:
                        for j in range(maps):
                            b = begin(sc[s, j])
                            for t in range(NT):
                                qs, ks = q_of(s, j), k_of(s, j)
                                for n in range(len(qs)):
                                    ins = pe.matmul(b[:, t * S:t * S + S], qs[n][:, t * P:t * P + P], ks[n],
                                                    start=n == 0, stop=n == len(qs) - 1)
                                    if t == 0:
                                        behind(ins)
                            end(ins, sc[s, j])
                    if s == 1 and between:
                        between()
                    if 2 <= s < heads + 2:
                        hd = s - 2
                        pe.wait_ge(probs, att_done[0] + hd + 1)
                        b = begin(tr[hd])
                        for k in range(NT):
                            for t in range(NT):
                                ins = pe.transpose(b[:, k * S + t * P:k * S + t * P + P],
                                                   prob(hd, 0, maps, t, k * P, P), ident)
                        end(ins, tr[hd])
                    if s >= 3:
                        hd = s - 3
                        moved(pe, tr[hd])
                        b = begin(ou[hd])
                        if by_tokens:
                            for t in range(NT):
                                for k in range(NT):
                                    ins = pe.matmul(b[:, t * P:t * P + P], pT[:, hd % 2, k, t * P:t * P + P],
                                                    values(hd, k), start=k == 0, stop=k == NT - 1)
                        else:
                            v = [values(hd, k) for k in range(NT)]
                            m = v[0].shape[1]
                            at = 64 * (hd % 2) if m == 64 else 0
                            for k in range(NT):
                                ins = pe.matmul(b[at:at + m, 0:S], v[k], pT[:, hd % 2, k, :],
                                                start=k == 0, stop=k == NT - 1)
                        end(ins, ou[hd])
                att_done[0] += heads

            att_done = [0]

            def outputs_moved(name):
                for g in attention_groups(name, G[name])[2].values():
                    moved(pe, g)

            X = (xh, xl)

            pe.wait_ge(s_const, 16)
            x_transposed("x0", 0)
            by_token(G["mla_down"], W["dq"], X, [5, 3], [QL])
            by_token(G["mla_down"] + 2, W["dkv"], X, [6, 2], [KVL + MR])
            keep_clock(12, begin(G["mla_t"]))
            for t in range(NT):
                pe.wait_ge(down_ready, t + 1)
                transposes(G["mla_t"] + t, [cqn[:, t, P * k:P * k + P] for k in range(3)])
            for t in range(NT):
                transposes(G["mla_t2"] + t, [ckvn[:, t, P * k:P * k + P] for k in range(2)] + [krr[:, t, :]])
            for t in range(NT):
                moved(pe, G["mla_t"] + t)
            for t in range(NT):
                begin(G["mla_qr"] + t)
            for n in range(4):
                p = W["uq"] + n
                pe.wait_ge(low_ready, p + 1)
                w = [y.rearrange("p k (h d) -> p k h d", d=MN + MR) for y in parts(p, 3, 384)]
                by_feature(G["mla_qn"] + n, [[y[:, :, x, 0:MN] for y in w] for x in range(2)], cq, 3)
                for t in range(NT):
                    for k in range(3):
                        _, ins = product(bank[(G["mla_qr"] + t) % 8][:, P * n:P * n + P].rearrange("p (h d) -> p h d", d=MR),
                                         [y[:, k, t * P:t * P + P] for y in cq], [y[:, k, :, MN:] for y in w],
                                         k == 0, k == 2)
                    if n == 3:
                        end(ins, G["mla_qr"] + t)
                owed[0] += 1
            for t in range(NT):
                moved(pe, G["mla_t2"] + t)
            for n in range(2):
                p = W["ukv"] + n
                pe.wait_ge(low_ready, p + 1)
                w = [y.rearrange("p k (h d) -> p k h d", d=2 * MN) for y in parts(p, 2, 1024)]
                for x in range(2):
                    by_feature(G["mla_kv"] + 4 * n + x, [[y[:, :, 2 * x + z, 0:MN] for y in w] for z in range(2)], ckv, 2)
                for t in range(NT):
                    g = G["mla_kv"] + 4 * n + 2 + t
                    b = begin(g)
                    for k in range(2):
                        _, ins = product(b[:, :].rearrange("p (h d) -> p h d", d=MN),
                                         [y[:, k, t * P:t * P + P] for y in ckv], [y[:, k, :, MN:] for y in w],
                                         k == 0, k == 1)
                    end(ins, g)
                owed[0] += 1
            for t in range(NT):
                pe.wait_ge(roped, t + 1)
                transposes(G["mla_qrt"] + t, [rr[:, t, P * k:P * k + P] for k in range(4)])
            attention("mla_att",
                      lambda s, j: [qT[:, s, :], qrT[64 * (s % 2):64 * (s % 2) + 64, s // 2, :]],
                      lambda s, j: [kT[:, s, :], krT[64 * (s % 2):64 * (s % 2) + 64, :]],
                      lambda hd, k: vtok[:, k, P * hd:P * hd + P], False,
                      range(G["mla_qn"], G["mla_att"]))
            pe.wait_ge(s_rows, 9 * 16)
            for l in range(2):
                transposes(G["par"] + l, [prow[0:88, 2 * l, :], prow[0:88, 1 + 2 * l, :]])
            transposes(G["par"] + 2, [prow[0:1, 4, :]])
            outputs_moved("mla_att")
            square_out("mla_o", W["mla_wo"], X)

            def ffn(l):
                b = W[f"ffn{l}"]
                n0 = l * FT

                def up(p, j, turn=0):
                    pe.wait_ge(low_ready, p + 1 + RING * turn)
                    w = [y[:, p % PARTS, :].rearrange("p (k a n) -> p k a n", a=2, n=P) for y in (high, low)]
                    for a in range(2):
                        for k in range(KT):
                            k_tile(k)
                            first, ins = product(bank[j % 4][:, a * S:a * S + S], [y[:, k, a, :] for y in w],
                                                 [y[:, k, :] for y in X], k == 0, k == KT - 1)
                            behind(first)
                    ins.then_inc(up_full, 1)
                    owed[0] += 1

                def down(p, j, n, turn=0, start=False, stop=False):
                    pe.wait_ge(low_ready, p + 1 + RING * turn)
                    w = parts(p, 2, D)
                    for x in range(2):
                        pe.wait_ge(hid_ready, n + (n0 + 1 + x))
                        for t in range(NT):
                            for hf in range(2):
                                first, ins = product(bank[4 + 2 * t + hf][:, :],
                                                     [y[:, (j + x) % 4, t * P:t * P + P] for y in (hh, hl)],
                                                     [y[:, x, 512 * hf:512 * hf + 512] for y in w],
                                                     start and x == 0, stop and x == 1)
                                behind(first)
                                if stop and x == 1:
                                    ins.then_inc(ffn_full, 1)
                    owed[0] += 1

                up(b, 0)
                up(b + 1, 1)
                for m in range(1, 3):
                    up(b + 3 * m - 1, 2 * m)
                    up(b + 3 * m, 2 * m + 1)
                    down(b + 3 * m + 1, 2 * m - 2, 2 * m - 2, start=m == 1)
                with pe.Fori(0, 4) as i:
                    for s in range(2):
                        up(b + 8 + 3 * s, 6 + 2 * s, i)
                        up(b + 9 + 3 * s, 7 + 2 * s, i)
                        down(b + 10 + 3 * s, 4 + 2 * s, 4 * i + (4 + 2 * s), i)
                down(b + 32, FT - 2, FT - 2, stop=True)

            keep_clock(WAIT, begin(G["x1"]))
            x_transposed("x1", 1)
            ffn(0)

            keep_clock(WAIT, bank[3])
            x_transposed("x2", 2)
            for n in range(8):
                pe.wait_ge(low_ready, W["qk"] + n + 1)
                w = parts(W["qk"] + n, KT, 256)
                by_feature(G["diff_q"] + n, [[y[:, :, P * x:P * x + P] for y in w] for x in range(2)], X, KT)
                owed[0] += 1

            def diff_values():
                for hf in range(2):
                    by_token(G["diff_v"] + 2 * hf, W["v"] + 2 * hf, X, [4, 4], [512])
                for g in range(4):
                    moved(pe, G["diff_v"] + g)

            attention("diff_att",
                      lambda s, j: [qT[64 * j:64 * j + 64, s, :]], lambda s, j: [kT[64 * j:64 * j + 64, s, :]],
                      lambda hd, k: vtok[:, k, P * hd:P * hd + P], True,
                      range(G["diff_q"], G["diff_att"]), diff_values)
            outputs_moved("diff_att")
            keep_clock(4, begin(G["diff_t"]))
            for t in range(NT):
                pe.wait_ge(o_ready, t + 1)
                for q in range(2):
                    transposes(G["diff_t"] + 2 * t + q, [otok[:, t, P * k:P * k + P] for k in range(4 * q, 4 * q + 4)])
            for g in range(4):
                moved(pe, G["diff_t"] + g)
            square_out("diff_o", W["diff_wo"], X)
            keep_clock(WAIT, begin(G["x3"]))
            x_transposed("x3", 3)
            ffn(1)

            keep_clock(WAIT, bank[3])
            x_transposed("x4", 4)
            n_rot = [NT]

            def columns(name):
                if name == "ki":
                    by_token(G[name], W[name], X, [8], [72])
                else:
                    by_token(G[name], W[name], X, [4, 4], [512])

            def rotated(name):
                for t in range(NT):
                    pe.wait_ge(roped, n_rot[0] + t + 1)
                    transposes(G[name + "_t"] + t, [rr[:, t, P * k:P * k + P] for k in range(1 if name == "ki" else 4)])
                n_rot[0] += NT

            columns("qi")
            columns("ki")
            rotated("qi")
            columns("qa")
            rotated("ki")
            for g in range(G["qi_t"], G["qi_t"] + 2):
                moved(pe, g)
            for g in range(G["ki_t"], G["ki_t"] + 2):
                moved(pe, g)
            for hd in range(8):
                b = begin(G["index"] + hd)
                at = 64 * (hd % 2)
                for t in range(NT):
                    ins = pe.matmul(b[:, t * S:t * S + S], qiT[at:at + 64, hd // 2, t * P:t * P + P],
                                    kiT[at:at + 64, :], start=True, stop=True)
                    if t == 0:
                        behind(ins)
                end(ins, G["index"] + hd)
            for kind, name in [(columns, "ka"), (rotated, "qa"), (columns, "va"), (rotated, "ka"), (columns, "qb"),
                               (columns, "kb"), (rotated, "qb"), (columns, "vb"), (rotated, "kb")]:
                kind(name)

            def halves(ap):
                return lambda s, j: [ap[64 * (s % 2):64 * (s % 2) + 64, s // 2, :]]

            def gates(a):
                for n in range(2):
                    by_token(G["g" + a] + 2 * n, W["g" + a] + 2 * n, X, [4, 4], [512])

            def projected(name, a, x):
                outputs_moved(name)
                square_out("p" + a, W["p" + a], x)

            def branch(name, a, q_, k_, v_, between):
                attention(name, halves(q_), halves(k_), lambda hd, k: v_[:, k, 64 * hd:64 * hd + 64], False,
                          [*range(G["q" + a + "_t"], G["q" + a + "_t"] + 2),
                           *range(G["k" + a + "_t"], G["k" + a + "_t"] + 2), *range(G["v" + a], G["v" + a] + 2)],
                          between)

            branch("moba_att", "a", qaT, kaT, va, lambda: gates("a"))
            gates("b")
            branch("dsa_att", "b", qbT, kbT, vb, lambda: projected("moba_att", "a", (hh, hl)))
            projected("dsa_att", "b", (xh[:, 0:4], xl[:, 0:4]))
            for t in range(NT):
                pe.wait_ge(mixed_ready, t + 1)
                for q in range(2):
                    transposes(G["mix_t"] + 2 * t + q, [siga[:, t, P * k:P * k + P] for k in range(4 * q, 4 * q + 4)])
            for g in range(4):
                moved(pe, G["mix_t"] + g)
            square_out("hyb_o", W["wout"], X)

            keep_clock(12, begin(G["x5"]))
            x_transposed("x5", 5)
            pe.wait_ge(s_gains, 16 * 5)
            pe.wait_ge(s_tables, 16)
            for t in range(NT):
                b = begin(G["router"] + t)
                for k in range(KT):
                    k_tile(k)
                    ins = pe.matmul(b[:, 0:NG + NE], xT[:, k, t * P:t * P + P], wr[:, k, :], start=k == 0, stop=k == KT - 1)
                end(ins, G["router"] + t)
            b = begin(G["pos"])
            keep_clock(24, b)
            pe.wait_ge(mask_ready, 1)
            tri, one = cs[:, C_TRI:C_TRI + P], cs[:, C_ONE:C_ONE + P]
            pe.matmul(b[:, 0:NE], tri, mask[:, 0, :], start=True, stop=True)
            pe.matmul(b[:, NE:2 * NE], one, mask[:, 0, :], start=True, stop=False)
            pe.matmul(b[:, NE:2 * NE], tri, mask[:, 1, :], start=False, stop=True)
            pe.matmul(b[:, 2 * NE:3 * NE], one, mask[:, 0, :], start=True, stop=False)
            end(pe.matmul(b[:, 2 * NE:3 * NE], one, mask[:, 1, :], start=False, stop=True), G["pos"])

            moved(pe, G["pos"])

            def gather(n, first=0, last=KT, frees=0):
                if first == 0:
                    pe.wait_ge(sel_ready, 1 + n)
                for k in range(first, last):
                    for t in range(NT):
                        ins = pe.matmul(bank[2 + k // 4][:, P * (k % 4):P * (k % 4) + P],
                                        xn[:, t, P * k:P * k + P], Sel[:, t].rearrange("p e c -> p (e c)"),
                                        start=t == 0, stop=t == NT - 1)
                        if k == 0 and t == 0 and frees:
                            ins.then_inc(halves_used, frees)
                    if k % 4 == 3:
                        ins.then_inc(xg_full, 1)

            def scatter(n, frees=0):
                pe.wait_ge(sgT_ready, 1 + n)
                pe.wait_ge(y_ready, 2 + 2 * n)
                for t in range(NT):
                    for hf in range(2):
                        ins = pe.matmul(bank[4 + 2 * t + hf][:, :], SgT[:, t, :], ysb[:, 512 * hf:512 * hf + 512],
                                        start=False, stop=False)
                        if t == 0 and hf == 0 and frees:
                            ins.then_inc(halves_used, frees)

            def pair(n, turn, first=False, opens=False, last=False):
                pe.wait_ge(xg_ready, 1 + 2 * n)
                if not first:
                    pe.wait_ge(y_ready, 2 * n)
                    pe.wait_ge(sgT_ready, n)
                for x, done in enumerate((h1_full, h3_full)):
                    if x and not opens:
                        scatter(n - 1, frees=2)
                    for k in range(KT):
                        if k == 4 and x == 0:
                            pe.wait_ge(xg_ready, 2 + 2 * n)
                        if k % 4 == 0:
                            have(pe, 2 * x, k // 4, turn)
                        for e in range(2):
                            ins = pe.matmul(bank[x][CAP * e:CAP * e + CAP, :], XgT[:, k, CAP * e:CAP * e + CAP],
                                            slot(2 * x + e, KT, EF)[:, k, :], start=k == 0, stop=k == KT - 1)
                            if e == 0 and (k == 4 or k == 0 and (opens if x else not first)):
                                ins.then_inc(halves_used, 2)
                    ins.then_inc(done, 1)
                if not last:
                    gather(n + 1, 0, 6, frees=2)
                if first:
                    pe.wait_ge(zeros_ready, 1)
                    for b in range(4, 8):
                        pe.matmul(bank[b][:, :], hh[:, 0, 0:P], hh[:, 0:2, :], start=True, stop=False)
                pe.wait_ge(hidden_ready, 1 + n)
                for k in range(4):
                    ins = pe.transpose(bank[0][:, P * k:P * k + P], hid[:, P * k:P * k + P], ident)
                    if k == 0 and last:
                        ins.then_inc(halves_used, 2)
                ins.then_inc(hidT_full, 1)
                if not last:
                    gather(n + 1, 6, KT)
                pe.wait_ge(hidT_ready, 1 + n)
                have(pe, 4, 0, turn)
                have(pe, 4, 1, turn)
                for hf in range(2):
                    if hf == 1:
                        pe.wait_ge(selg_ready, 1 + n)
                        for t in range(NT):
                            ins = pe.transpose(bank[0][:, P * t:P * t + P],
                                               SelG[:, t].rearrange("p e c -> p (e c)"), ident)
                        ins.then_inc(sgT_full, 1)
                        if not last:
                            pe.wait_ge(xg_ready, 4 + 2 * n)
                    for k in range(4):
                        for e in range(2):
                            ins = pe.matmul(bank[1 + hf][CAP * e:CAP * e + CAP, :], hidT[:, k, CAP * e:CAP * e + CAP],
                                            slot(4 + e, 4, D)[:, k, 512 * hf:512 * hf + 512],
                                            start=k == 0, stop=k == 3)
                            if hf == 1 and k == 2 and e == 0:
                                ins.then_inc(halves_used, 2)
                    ins.then_inc(y_full, 1)

            gather(0)
            pair(0, 0, first=True, opens=True)
            with pe.Fori(1, NP - 1) as i:
                pair(i, i)
            pair(NP - 1, NP - 1, last=True)
            scatter(NP - 1)
            pe.wait_ge(flag_ready, 1)
            over = pe.value_load(flag[0:1, 0:1], min_val=0, max_val=1)
            with pe.If(over):
                with pe.Fori(1, ROUNDS) as r:
                    gather(r * NP)
                    pair(r * NP, r * NP, opens=True)
                    with pe.Fori(1, NP - 1) as i:
                        pair(r * NP + i, r * NP + i)
                    pair(r * NP + (NP - 1), r * NP + (NP - 1), last=True)
                    scatter(r * NP + (NP - 1))
            for b in range(4, 8):
                pe.matmul(bank[b][:, :], hh[:, 0, 0:P], hh[:, 0:2, :], start=False, stop=True).then_inc(moe_full, 1)

        @block.scalar
        def _(act):
            ready = [0]

            def high_of(p, n=PIECE, turn=0):
                act.wait_ge(piece_here[p % RING], 32 * (p // RING + 1) + 32 * turn)
                if p >= PARTS:
                    act.wait_ge(pieces_used, p - PARTS + 1 + RING * turn)
                act.activation(high[:, p % PARTS, 0:n], raw[:, p % RING, 0:n], ACT.Copy).then_inc(high_ready, 1)

            def split(last):
                while ready[0] <= min(last, W["end"] - 1):
                    high_of(ready[0], WIDTH[ready[0]])
                    ready[0] += 1

            def squares(dst, src, junk, done):
                act.activation(junk, src, ACT.Square, accum_out=dst).then_inc(done, 1)

            def h_sums(site):
                for t in range(NT):
                    if site == 0:
                        act.wait_ge(s_x, 32)
                    else:
                        act.wait_ge(h_ready, 2 * (site - 1) + t + 1)
                    squares(st[:, t:t + 1], h[:, t, :], xn[:, t, :], h_squares)
                act.wait_ge(h_squares, 2 * site + 2)
                guess(st[:, 16:18], st[:, 0:2], D)

            def guess(dst, sums, width):
                act.activation(dst, sums, ACT.Abs_reciprocal_sqrt, bias=eps_t[:, 0:1],
                               scale=1.0 / width).then_inc(guessed, 1)

            loads = [0]

            def load_table(func):
                loads[0] += 1
                act.activation(eps_t[:, loads[0]:loads[0] + 1], eps_t[:, 0:1], func)

            def copy(g, dst, src, func=ACT.Copy):
                full(act, g)
                act.activation(dst, src, func).then_inc(bank_moved[g % 8], 1)

            def high_part(g, dst, src, scale=1.0):
                full(act, g)
                act.activation(dst, src, ACT.Copy, scale=scale).then_inc(x_high, 1)

            def high_tiles(name, order, n, first=0, scale=1.0):
                for x, (t, q) in enumerate(order):
                    g = G[name] + x
                    high_part(g, xh[:, first + n * q:first + n * q + n, t * P:t * P + P],
                              bank[g % 8][:, 0:n * P].rearrange("p (a b) -> p a b", b=P), scale)

            def tiles(g, dst, t, n):
                copy(g, dst[:, 0:n, t * P:t * P + P], bank[g % 8][:, 0:n * P].rearrange("p (a b) -> p a b", b=P))

            def out_sums(banks):
                for n, (b, wait) in enumerate(banks):
                    wait(act)
                    if n == 0:
                        outs_done[0] += 1
                    squares(st[:, 2 + n:3 + n], bank[b][:, :], view(6400 + 512 * n, 512), post_squares)
                act.wait_ge(sums_ready, outs_done[0])
                guess(st[:, 16:18], st[:, 18:20], D)

            outs_done = [0]

            def group_banks(g0):
                return [((g0 + n) % 8, lambda e, g=g0 + n: full(e, g)) for n in range(4)]

            def ffn_banks(l):
                return [(4 + n, lambda e, n=n: e.wait_ge(ffn_full, 4 * l + n + 1)) for n in range(4)]

            heads_done = [0]

            def attention(name, scale, biased, output, between=None):
                heads, maps, _ = STAGES[name]
                sc, tr, ou, _ = attention_groups(name, G[name])
                for s in range(heads + 3):
                    c = s % 2
                    if s < heads:
                        act.wait_ge(neg_max, heads_done[0] + s + 1)
                        if maps == 2 and s >= 2:
                            full(act, tr[s - 2])
                        for j in range(maps):
                            for t in range(NT):
                                src = sc_sb[:, c, j, t, :] if biased else bank[sc[s, 0] % 8][:, t * S:t * S + S]
                                ins = act.activation(prob(s, j, maps, t), src, ACT.Exp,
                                                     bias=att[:, 1, c, j, t:t + 1], scale=scale,
                                                     accum_out=att[:, 2, c, j, t:t + 1])
                                if biased:
                                    ins.then_inc(exped, 1)
                                elif t == NT - 1:
                                    ins.then_inc(bank_moved[sc[s, 0] % 8], 1)
                    if s == 1 and between:
                        between()
                    if s == heads and name != "moba_att":
                        load_table(ACT.Abs_reciprocal_sqrt)
                    if 2 <= s < heads + 2:
                        g = tr[s - 2]
                        copy(g, pT[:, s % 2].rearrange("p k q -> p (k q)"), bank[g % 8][:, :])
                    if s >= 3:
                        output(ou[s - 3], s - 3, bank[ou[s - 3] % 8])
                heads_done[0] += heads

            act.wait_ge(eps_set, 1)
            load_table(ACT.Abs_reciprocal_sqrt)
            h_sums(0)
            split(1)
            high_tiles("x0", HALVES, 4)
            split(W["dkv"] + 1)
            for t in range(NT):
                full(act, G["mla_down"] + t)
                squares(st[:, 6 + t:7 + t], bank[(G["mla_down"] + t) % 8][:, 0:QL], view(6144 + QL * t, QL), down_squares)
            act.wait_ge(down_squares, 2)
            guess(st[:, 20:22], st[:, 6:8], QL)
            split(W["uq"] + 1)
            for t in range(NT):
                full(act, G["mla_down"] + 2 + t)
                squares(st[:, 8 + t:9 + t], bank[(G["mla_down"] + 2 + t) % 8][:, 0:KVL],
                        view(6144 + 2 * QL + KVL * t, KVL), down_squares)
            act.wait_ge(down_squares, 4)
            guess(st[:, 22:24], st[:, 8:10], KVL)
            high_tiles("mla_t", TILES, 3)
            high_tiles("mla_t2", TILES, 2, first=3)
            for x in range(4):
                split(W["uq"] + x + 2)
                g = G["mla_qn"] + x
                copy(g, view(512 * x, 512), bank[g % 8][:, :])
            for n in range(2):
                split(W["ukv"] + n + 2)
                for x in range(2):
                    g = G["mla_kv"] + 4 * n + x
                    copy(g, view(2048 + 512 * (2 * n + x), 512), bank[g % 8][:, :])
                for t in range(NT):
                    g = G["mla_kv"] + 4 * n + 2 + t
                    copy(g, vtok[:, t, 512 * n:512 * n + 512], bank[g % 8][:, :])
            for t in range(NT):
                tiles(G["mla_qrt"] + t, qrT, t, 4)
            split(W["ukv"] + 4)
            attention("mla_att", MLA_SCALE, False, lambda g, hd, b: high_part(g, xh[:, hd, :], b[:, 0:S]))
            split(W["mla_wo"] + 5)
            out_sums(group_banks(G["mla_o"]))

            def tile(n, b, par):
                act.wait_ge(up_full, 1 + n)
                for a in range(2):
                    act.activation(fbuf[b][a], bank[b][:, a * S:a * S + S], ACT.Identity,
                                   bias=par(3, a), scale=par(1, a)).then_inc(centre, 1)
                act.wait_ge(conv_done, 1 + n)
                act.activation(fbuf[b][2], fbuf[b][0], ACT.Square, scale=0.044715 ** 0.5).then_inc(g_squared, 1)
                act.wait_ge(g_inner, 1 + n)
                act.activation(fbuf[b][5], fbuf[b][3], ACT.Tanh, scale=(2 / np.pi) ** 0.5).then_inc(tanhed, 1)

            def ffn(l):
                b = W[f"ffn{l}"]
                n0 = l * FT
                for m in range(3):
                    for x in range(2):
                        j = 2 * m + x
                        split(b + 3 * m + 2 + x)
                        tile(n0 + j, j % 4, lambda w, a: convT[:, l, w, a, j:j + 1])
                    split(b + 3 * m + 4)
                with act.Fori(0, 4) as i:
                    for s in range(2):
                        for x in range(2):
                            high_of(b + 11 + 3 * s + x, turn=i)
                            if s == 0 and x == 0:
                                act.wait_ge(params_set, i + (4 * l + 1))
                            j = 2 * s + x
                            tile(4 * i + (n0 + 6 + j), (6 + j) % 4, lambda w, a: cpar[:, w, a, j:j + 1])
                        high_of(b + 13 + 3 * s, turn=i)
                ready[0] = b + 3 * FM + 2

            h_sums(1)
            high_tiles("x1", HALVES, 4)
            ffn(0)
            load_table(ACT.Abs_reciprocal_sqrt)
            out_sums(ffn_banks(0))

            h_sums(2)
            high_tiles("x2", HALVES, 4)
            act.wait_ge(lam_dots, 1)
            act.activation(st[:, 12:14], st[:, 10:12], ACT.Exp).then_inc(lam_exps, 1)
            for x in range(8):
                split(min(W["qk"] + x + 3, W["v"] + 1))
                g = G["diff_q"] + x
                copy(g, view(512 * x, 512), bank[g % 8][:, :])
            split(W["v"] + 2)

            def diff_values():
                for hf in range(2):
                    split(W["v"] + 2 * hf + 3)
                    for t in range(NT):
                        g = G["diff_v"] + 2 * hf + t
                        copy(g, vtok[:, t, 512 * hf:512 * hf + 512], bank[g % 8][:, :])
                split(W["v"] + 6)

            def head_out(g, hd, b):
                full(act, g)
                for t in range(NT):
                    act.activation(xl[:, hd, t * P:t * P + P], b[:, t * P:t * P + P], ACT.Square,
                                   accum_out=ss_o[:, 8 * t + hd:8 * t + hd + 1])
                copy(g, otok[:, :, P * hd:P * hd + P], b[:, 0:S].rearrange("p (t d) -> p t d", t=NT))

            attention("diff_att", HD_SCALE, True, head_out, diff_values)
            g = list(attention_groups("diff_att", G["diff_att"])[2].values())[-1]
            moved(act, g)
            guess(rs_o[:, 0:16], ss_o[:, 0:16], P)
            act.wait_ge(o_ready, 1)
            high_tiles("diff_t", TILE_HALVES, 4, scale=st[:, 15:16])
            split(W["diff_wo"] + 5)
            out_sums(group_banks(G["diff_o"]))
            h_sums(3)
            high_tiles("x3", HALVES, 4)
            ffn(1)
            load_table(ACT.Abs_reciprocal_sqrt)
            out_sums(ffn_banks(1))

            h_sums(4)
            high_tiles("x4", HALVES, 4)
            split(W["ki"] + 2)
            for t in range(NT):
                tiles(G["qi_t"] + t, qiT, t, 4)
            split(W["qa"] + 3)
            for t in range(NT):
                g = G["ki_t"] + t
                copy(g, kiT[:, t * P:t * P + P], bank[g % 8][:, 0:P])
            split(W["qa"] + 4)
            for hd in range(8):
                if hd >= 2:
                    act.wait_ge(scored, hd - 1)
                g = G["index"] + hd
                full(act, g)
                act.activation(relu[:, hd % 2, :], bank[g % 8][:, :], ACT.Relu).then_inc(bank_moved[g % 8], 1)
            for name, behind, dst in [("qa", "ka", qaT), ("va", "va", va), ("ka", "va", kaT),
                                      ("qb", "kb", qbT), ("vb", "vb", vb), ("kb", "vb", kbT)]:
                split(W[behind] + 3)
                for t in range(NT):
                    if name[0] == "v":
                        g = G[name] + t
                        copy(g, dst[:, t, :], bank[g % 8][:, :])
                    else:
                        tiles(G[name + "_t"] + t, dst, t, 4)

            def gates(a, sig):
                for n in range(2):
                    split(W["g" + a] + 2 * n + 3)
                    for t in range(NT):
                        g = G["g" + a] + 2 * n + t
                        copy(g, sig[:, t, 512 * n:512 * n + 512], bank[g % 8][:, :], ACT.Sigmoid)
                split(W["g" + a] + 6)

            def half_heads(o):
                def one(g, hd, b):
                    at = 64 * (hd % 2)
                    high_part(g, o[at:at + 64, hd // 2, :], b[at:at + 64, 0:S])
                return one

            split(W["ga"] + 2)
            attention("moba_att", HD_SCALE, True, half_heads(hh), lambda: gates("a", siga))
            gates("b", sigb)
            attention("dsa_att", HD_SCALE, True, half_heads(xh), lambda: split(W["pb"] + 2))
            split(W["pb"] + 3)
            high_tiles("mix_t", TILE_HALVES, 4)
            split(W["end"])
            h_sums(5)
            for t in range(NT):
                tiles(G["x5"] + t, xT, t, 4)

            load_table(ACT.Exp)

            act.activation(hh[:, 0:2, :], cs[:, 0:2 * S].rearrange("p (a b) -> p a b", b=S), ACT.Copy,
                           scale=0.0).then_inc(zeros_ready, 1)
            for n in range(2):
                act.wait_ge(logits_max, n + 1)
                act.activation(r_exp[n], r_dif[n], ACT.Exp).then_inc(logits_exp, 1)

            def pair(n):
                act.wait_ge(h1_full, 1 + n)
                act.activation(silu, bank[0][:, :], ACT.Silu).then_inc(silu_ready, 1)
                act.wait_ge(hidT_full, 1 + n)
                act.activation(hidT.rearrange("p a b -> p (a b)"), bank[0][:, :], ACT.Copy).then_inc(hidT_ready, 1)
                for hf in range(2):
                    act.wait_ge(y_full, 2 * n + (1 + hf))
                    act.activation(ysb[:, 512 * hf:512 * hf + 512], bank[1 + hf][:, :], ACT.Copy).then_inc(y_ready, 1)

            with act.Fori(0, NP) as i:
                pair(i)
            act.wait_ge(flag_ready, 1)
            over = act.value_load(flag[0:1, 0:1], min_val=0, max_val=1)
            with act.If(over):
                with act.Fori(NP, ROUNDS * NP) as n:
                    pair(n)
            h_sums(6)

        @block.vector
        def _(dve):
            steps = [0]

            def link(ins):
                steps[0] += 1
                ins.then_inc(vec, 1)
                dve.wait_ge(vec, steps[0])

            def refined(dst, src, width=D, n=2):
                v2, a = st[:, 32:32 + n], st[:, 48:48 + n]
                dve.tensor_scalar(v2, src, -0.5 / width, -0.5 * EPS, ALU.mult, ALU.add)
                guesses[0] += 1
                dve.wait_ge(guessed, guesses[0])
                link(dve.tensor_tensor(a, dst, dst, ALU.mult))
                link(dve.tensor_tensor(a, a, v2, ALU.mult))
                link(dve.scalar_tensor_tensor(dst, a, 1.5, dst, ALU.add, ALU.mult))

            guesses = [0]

            def spread(ap, *shape):
                return ap.unsqueeze(len(ap.shape)).to_broadcast([P, *shape])

            def blocks(ap, n):
                return ap[:, 0:n * P].rearrange("p (a b) -> p a b", b=P)

            x_parts = [0]

            def low_part(g, low_, high_, src, scale=None):
                x_parts[0] += 1
                dve.wait_ge(x_high, x_parts[0])
                if scale is None:
                    ins = dve.tensor_tensor(low_, src, high_, ALU.subtract)
                else:
                    ins = dve.scalar_tensor_tensor(low_, src, scale, high_, ALU.mult, ALU.subtract)
                ins.then_inc(bank_moved[g % 8], 1)

            def low_tiles(name, order, n, first=0, scale=None):
                for i, (t, q) in enumerate(order):
                    g = G[name] + i
                    x = [y[:, first + n * q:first + n * q + n, t * P:t * P + P] for y in (xl, xh)]
                    low_part(g, x[0], x[1], blocks(bank[g % 8], n), scale)

            def normed(site):
                dve.wait_ge(h_squares, 2 * site + 2)
                refined(st[:, 16:18], st[:, 0:2])
                dve.wait_ge(gpre_here, 16 * (site + 1))
                for t, q in HALVES:
                    x = slice(512 * q, 512 * q + 512)
                    dve.scalar_tensor_tensor(xn[:, t, x], h[:, t, x], st[:, 16 + t:17 + t], gpre[:, x],
                                             ALU.mult, ALU.mult).then_inc(xn_ready, 1)

            def x_transposed(name, site):
                normed(site)
                low_tiles(name, HALVES, 4)

            def post(site, banks, ring_groups):
                dve.wait_ge(gpost_here, 16 * (site + 1))
                for n, b in enumerate(banks):
                    t, hf = divmod(n, 2)
                    dve.wait_ge(post_squares, 4 * site + n + 1)
                    ins = dve.tensor_tensor(xn[:, t, 512 * hf:512 * hf + 512], bank[b][:, :],
                                            gpost[:, 512 * hf:512 * hf + 512], ALU.mult)
                    ins.then_inc(bank_moved[b] if ring_groups else vec, 1)
                if not ring_groups:
                    steps[0] += 4
                sums = st[:, 2:6].rearrange("p (t h) -> p t h", h=2)
                dve.tensor_tensor(st[:, 18:20], sums[:, :, 0], sums[:, :, 1], ALU.add).then_inc(sums_ready, 1)
                dve.wait_ge(sums_ready, site + 1)
                refined(st[:, 16:18], st[:, 18:20])
                for g in ring_groups or []:
                    moved(dve, g)
                for t in range(NT):
                    dve.scalar_tensor_tensor(h[:, t, :], xn[:, t, :], st[:, 16 + t:17 + t], h[:, t, :],
                                             ALU.mult, ALU.add).then_inc(h_ready, 1)

            rotations = {}

            def rope(g, t, nh, dst=None, done=roped, off=0):
                if rotations:
                    last = rotations["last"]
                    dve.wait_ge(last, rotations[last.name])
                rotations[done.name] = rotations.get(done.name, 0) + 1
                rotations["last"] = done
                src = bank[g % 8][:, off:off + nh * HD].rearrange("p (h two d) -> p h two d", two=2, d=32)
                t1 = rt[:, 0, 0:nh * HD].rearrange("p (h d) -> p h d", d=HD)
                t2 = rt[:, 1, 0:nh * HD].rearrange("p (h two d) -> p h two d", two=2, d=32)
                cb = cos[:, t, :].unsqueeze(1).to_broadcast([P, nh, HD])
                dve.tensor_tensor(t1, bank[g % 8][:, off:off + nh * HD].rearrange("p (h d) -> p h d", d=HD), cb, ALU.mult)
                for y in range(2):
                    sb_ = sin[:, t, 32 * y:32 * y + 32].unsqueeze(1).to_broadcast([P, nh, 32])
                    ins = dve.tensor_tensor(t2[:, :, y, :], src[:, :, 1 - y, :], sb_, ALU.mult)
                ins.then_inc(bank_moved[g % 8], 1)
                moved(dve, g)
                if dst is None:
                    dve.tensor_tensor(rr[:, t, 0:nh * HD], rt[:, 0, 0:nh * HD], rt[:, 1, 0:nh * HD],
                                      ALU.add).then_inc(roped, 1)
                else:
                    a, b = (rt[:, y, 0:HD].unsqueeze(1).to_broadcast([P, 2, HD]) for y in range(2))
                    dve.tensor_tensor(dst, a, b, ALU.add).then_inc(done, 1)

            exps_done = [0]

            def attention(name, scale, bias=None, output=None, between=None):
                heads, maps, _ = STAGES[name]
                sc, tr, ou, _ = attention_groups(name, G[name])
                for s in range(heads + 4):
                    if s < heads:
                        c = s % 2
                        for j in range(maps):
                            g = sc[s, j]
                            full(dve, g)
                            src = bank[g % 8][:, :].rearrange("p (t k) -> p t k", t=NT)
                            if bias:
                                ap, factor = bias(s)
                                dve.scalar_tensor_tensor(sc_sb[:, c, j], ap, factor, src, ALU.mult,
                                                         ALU.add).then_inc(bank_moved[g % 8], 1)
                                moved(dve, g)
                                src = sc_sb[:, c, j]
                            link(dve.tensor_reduce(att[:, 0, c, j, :], src, AX, ALU.max))
                        dve.tensor_scalar(att[:, 1, c, 0:maps, :], att[:, 0, c, 0:maps, :], -scale, None,
                                          ALU.mult).then_inc(neg_max, 1)
                    if s >= 4 and output:
                        output(ou[s - 4], s - 4, bank[ou[s - 4] % 8])
                    if 1 <= s <= heads:
                        hd, c = s - 1, (s - 1) % 2
                        if bias:
                            exps_done[0] += NT * maps
                            dve.wait_ge(exped, exps_done[0])
                        else:
                            moved(dve, sc[hd, 0])
                        link(dve.reciprocal(att[:, 3, c, 0:maps, :], att[:, 2, c, 0:maps, :]))
                        if maps == 2:
                            link(dve.tensor_scalar(att[:, 3, c, 1, :], att[:, 3, c, 1, :], st[:, 14:15], None, ALU.mult))
                            for t in range(NT):
                                p1 = prob(hd, 1, maps, t)
                                ins = dve.tensor_scalar(p1, p1, att[:, 3, c, 1, t:t + 1], None, ALU.mult)
                            link(ins)
                        for t in range(NT):
                            p0, r0 = prob(hd, 0, maps, t), att[:, 3, c, 0, t:t + 1]
                            if maps == 2:
                                ins = dve.scalar_tensor_tensor(p0, p0, r0, prob(hd, 1, maps, t), ALU.mult, ALU.add)
                            else:
                                ins = dve.tensor_scalar(p0, p0, r0, None, ALU.mult)
                        ins.then_inc(probs, 1)
                    if s == 1 and between:
                        between()

            dve.memset(eps_t[:, 0:1], EPS).then_inc(eps_set, 1)
            x_transposed("x0", 0)
            dve.wait_ge(s_tables, 16)
            g = G["mla_down"]
            dve.wait_ge(down_squares, 2)
            refined(st[:, 20:22], st[:, 6:8], QL)
            dve.wait_ge(s_mla, 32)
            for t in range(NT):
                dve.scalar_tensor_tensor(cqn[:, t, :], bank[(g + t) % 8][:, 0:QL], st[:, 20 + t:21 + t],
                                         gpost[:, 0:QL], ALU.mult, ALU.mult).then_inc(bank_moved[(g + t) % 8], 1)
            dve.wait_ge(down_squares, 4)
            refined(st[:, 22:24], st[:, 8:10], KVL)
            for t in range(NT):
                dve.scalar_tensor_tensor(ckvn[:, t, :], bank[(g + 2 + t) % 8][:, 0:KVL], st[:, 22 + t:23 + t],
                                         gpost[:, QL:QL + KVL], ALU.mult, ALU.mult)
                rope(g + 2 + t, t, 1, krr[:, t, :].rearrange("p (a b) -> p a b", a=2), down_ready, off=KVL)
            low_tiles("mla_t", TILES, 3)
            for t in range(NT):
                g = G["mla_t2"] + t
                dve.wait_ge(x_high, x_parts[0] + 1)
                dve.tensor_copy(krT[:, t * P:t * P + P], bank[g % 8][:, 2 * P:3 * P])
                x = [y[:, 3:5, t * P:t * P + P] for y in (xl, xh)]
                low_part(g, x[0], x[1], blocks(bank[g % 8], 2))
            for t in range(NT):
                full(dve, G["mla_qr"] + t)
                rope(G["mla_qr"] + t, t, MH)
            attention("mla_att", MLA_SCALE,
                      output=lambda g, hd, b: low_part(g, xl[:, hd, :], xh[:, hd, :], b[:, 0:S]))
            for l in range(2):
                g = G["par"] + l
                full(dve, g)
                dve.tensor_copy(convT[:, l].rearrange("p a b c -> p (a b c)"),
                                bank[g % 8][:, 0:8 * FT]).then_inc(bank_moved[g % 8], 1)
            g = G["par"] + 2
            full(dve, g)
            dve.tensor_copy(subT[:, :], bank[g % 8][:, 0:1]).then_inc(bank_moved[g % 8], 1)
            for g in range(G["par"], G["par"] + 3):
                moved(dve, g)
            post(0, [(G["mla_o"] + n) % 8 for n in range(4)], range(G["mla_o"], G["mla_o"] + 4))

            def tile(n, b, par):
                x, u = [fbuf[b][a] for a in range(2)], [bank[b][:, a * S:a * S + S] for a in range(2)]
                dve.wait_ge(centre, 2 * n + 2)
                for a in range(2):
                    ins = dve.scalar_tensor_tensor(x[a][:, 1:S], u[a][:, 0:S - 1], par(0, a), x[a][:, 1:S],
                                                   ALU.mult, ALU.add)
                ins.then_inc(conv_step, 1)
                dve.wait_ge(conv_step, n + 1)
                for a in range(2):
                    ins = dve.scalar_tensor_tensor(x[a][:, 0:S - 1], u[a][:, 1:S], par(2, a), x[a][:, 0:S - 1],
                                                   ALU.mult, ALU.add)
                ins.then_inc(conv_done, 1)
                dve.wait_ge(g_squared, n + 1)
                dve.scalar_tensor_tensor(fbuf[b][3], fbuf[b][2], 1.0, x[0], ALU.add, ALU.mult).then_inc(g_inner, 1)
                dve.wait_ge(tanhed, n + 1)
                dve.scalar_tensor_tensor(fbuf[b][2], fbuf[b][5], 1.0, x[0], ALU.add, ALU.mult).then_inc(g_half, 1)
                dve.wait_ge(g_half, n + 1)
                dve.scalar_tensor_tensor(fbuf[b][4], fbuf[b][2], 0.5, x[1], ALU.mult, ALU.mult)
                dve.scalar_tensor_tensor(hh[:, b, :], fbuf[b][2], 0.5, x[1], ALU.mult, ALU.mult).then_inc(hid_high, 1)
                dve.wait_ge(hid_high, n + 1)
                dve.tensor_tensor(hl[:, b, :], fbuf[b][4], hh[:, b, :], ALU.subtract).then_inc(hid_ready, 1)

            def ffn(l):
                for j in range(6):
                    tile(l * FT + j, j % 4, lambda w, a: convT[:, l, w, a, j:j + 1])
                with dve.Fori(0, 4) as i:
                    dve.tensor_copy(cpar[:, :, :, :], convT[:, l, :, :, bass.ds(4 * i + 6, 4)]).then_inc(params_set, 1)
                    dve.wait_ge(params_set, i + (4 * l + 1))
                    for x in range(4):
                        tile(4 * i + (l * FT + 6 + x), (6 + x) % 4, lambda w, a: cpar[:, w, a, x:x + 1])

            x_transposed("x1", 1)
            ffn(0)
            post(1, range(4, 8), None)

            x_transposed("x2", 2)
            dve.wait_ge(s_gains, 5 * 16)
            lv = lamp[:, :, :].rearrange("p (a b) d -> p a b d", b=2)
            lp = scratch[:, 0:2 * HD].rearrange("p (a d) -> p a d", a=2)
            link(dve.tensor_tensor(lp, lv[:, :, 0, :], lv[:, :, 1, :], ALU.mult))
            dve.tensor_reduce(st[:, 10:12], lp, AX, ALU.add).then_inc(lam_dots, 1)
            dve.wait_ge(lam_exps, 1)
            link(dve.tensor_tensor(st[:, 14:15], st[:, 12:13], st[:, 13:14], ALU.subtract))
            link(dve.tensor_scalar(st[:, 14:15], st[:, 14:15], LAM_INIT, -1.0, ALU.add, ALU.mult))
            link(dve.tensor_scalar(st[:, 15:16], subT[:, :], 1.0 - LAM_INIT, None, ALU.mult))
            attention("diff_att", HD_SCALE, lambda s: (dist, -(2.0 ** -(s + 1.0)) / HD_SCALE))
            for g in attention_groups("diff_att", G["diff_att"])[2].values():
                moved(dve, g)
            refined(rs_o[:, 0:16], ss_o[:, 0:16], P, 16)
            for t in range(NT):
                o3 = otok[:, t].rearrange("p (h d) -> p h d", d=P)
                dve.tensor_tensor(o3, o3, spread(rs_o[:, 8 * t:8 * t + 8], 8, P), ALU.mult).then_inc(o_ready, 1)
            low_tiles("diff_t", TILE_HALVES, 4, scale=st[:, 15:16])
            post(2, [(G["diff_o"] + n) % 8 for n in range(4)], range(G["diff_o"], G["diff_o"] + 4))
            x_transposed("x3", 3)
            ffn(1)
            post(3, range(4, 8), None)

            x_transposed("x4", 4)
            for t in range(NT):
                full(dve, G["qi"] + t)
                rope(G["qi"] + t, t, 8)
            for t in range(NT):
                g = G["ki"] + t
                full(dve, g)
                full(dve, G["qi_t"] + t)
                dve.tensor_scalar(wi[:, t, :], bank[g % 8][:, HD:HD + 8], IDX_SCALE, None, ALU.mult)
                rope(g, t, 1, rr[:, t, 0:P].rearrange("p (a b) -> p a b", a=2), roped)

            def rotate(name, last):
                for t in range(NT):
                    full(dve, G[name] + t)
                    full(dve, G[last + "_t"] + t)
                    rope(G[name] + t, t, 8)

            rotate("qa", "ki")
            for hd in range(8):
                moved(dve, G["index"] + hd)
                for t in range(NT):
                    r_ = relu[:, hd % 2, t * S:t * S + S]
                    if hd == 0:
                        ins = dve.tensor_scalar(score[:, t, :], r_, wi[:, t, 0:1], None, ALU.mult)
                    else:
                        ins = dve.scalar_tensor_tensor(score[:, t, :], r_, wi[:, t, hd:hd + 1], score[:, t, :],
                                                       ALU.mult, ALU.add)
                ins.then_inc(scored, 1)
                dve.wait_ge(scored, hd + 1)
            link(dve.tensor_tensor(score[:, :, :], score[:, :, :], caus, ALU.add))
            for name, last in [("ka", "qa"), ("qb", "ka"), ("kb", "qb")]:
                rotate(name, last)

            def output(low_, high_):
                def one(g, hd, b):
                    at = 64 * (hd % 2)
                    low_part(g, low_[at:at + 64, hd // 2, :], high_[at:at + 64, hd // 2, :], b[at:at + 64, 0:S])
                return one

            attention("moba_att", HD_SCALE, lambda s: (caus, 1.0), output(hl, hh))
            for r in range(TOPK // 8):
                for t in range(NT):
                    ins = dve.max(top8[:, t, :], work[r % 2][:, t, :])
                link(ins)
                for t in range(NT):
                    ins = dve.match_replace(work[1 - r % 2][:, t, :], top8[:, t, :], work[r % 2][:, t, :], -3e38)
                link(ins)
            link(dve.tensor_scalar(selm, work[0], -2e38, -NEG, ALU.is_le, ALU.mult))
            link(dve.scalar_tensor_tensor(selm, selm, NEG, caus, ALU.add, ALU.add))

            def gate_a():
                for g in range(G["ga"], G["ga"] + 4):
                    moved(dve, g)
                for t in range(NT):
                    for hf in range(2):
                        g = G["pa"] + 2 * t + hf
                        full(dve, g)
                        x = siga[:, t, 512 * hf:512 * hf + 512]
                        dve.tensor_tensor(x, bank[g % 8][:, :], x, ALU.mult).then_inc(bank_moved[g % 8], 1)

            attention("dsa_att", HD_SCALE, lambda s: (selm, 1.0), output(xl, xh), gate_a)
            for g in range(G["gb"], G["gb"] + 4):
                moved(dve, g)
            for t in range(NT):
                for hf in range(2):
                    g = G["pb"] + 2 * t + hf
                    full(dve, g)
                    dve.tensor_tensor(mtmp[:, 2 * t + hf, :], bank[g % 8][:, :], sigb[:, t, 512 * hf:512 * hf + 512],
                                      ALU.mult).then_inc(bank_moved[g % 8], 1)
                for hf in range(2):
                    moved(dve, G["pa"] + 2 * t + hf)
                    moved(dve, G["pb"] + 2 * t + hf)
                dve.tensor_tensor(siga[:, t, :], siga[:, t, :],
                                  mtmp[:, 2 * t:2 * t + 2, :].rearrange("p a b -> p (a b)"), ALU.add).then_inc(mixed_ready, 1)
            low_tiles("mix_t", TILE_HALVES, 4)
            for t in range(NT):
                for hf in range(2):
                    g = G["hyb_o"] + 2 * t + hf
                    full(dve, g)
                    x = h[:, t, 512 * hf:512 * hf + 512]
                    dve.tensor_tensor(x, x, bank[g % 8][:, :], ALU.add).then_inc(bank_moved[g % 8], 1)
                moved(dve, G["hyb_o"] + 2 * t + 1)
                dve.tensor_copy(st[:, 24:25], h[:, t, 0:1]).then_inc(h_ready, 1)

            normed(5)
            for t in range(NT):
                g = G["x5"] + NT + t
                full(dve, g)
                dve.tensor_copy(xT[:, 4:8, t * P:t * P + P], blocks(bank[g % 8], 4)).then_inc(bank_moved[g % 8], 1)
            link(dve.tensor_scalar(w8, cs[:, C_IOTA:C_IOTA + 8], -1.0, 8.0, ALU.mult, ALU.add))
            for t in range(NT):
                g = G["router"] + t
                full(dve, g)
                dve.tensor_tensor(lg[:, t, :], bank[g % 8][:, 0:NG + NE], br[:, :], ALU.add).then_inc(bank_moved[g % 8], 1)
                moved(dve, g)

            def minus_max(dst, src, top, n):
                link(dve.tensor_reduce(top, src, AX, ALU.max))
                return dve.tensor_tensor(dst, src, spread(top, NT, n), ALU.subtract)

            def first_max(hot, dif, top, n):
                w = w8[:, 0:n].unsqueeze(1).to_broadcast([P, NT, n])
                link(dve.scalar_tensor_tensor(hot, dif, 0.0, w, ALU.is_equal, ALU.mult))
                link(dve.tensor_reduce(top, hot, AX, ALU.max))
                link(dve.tensor_tensor(hot, hot, spread(top, NT, n), ALU.is_equal))

            minus_max(r_dif[0], lg[:, :, 0:NG], r_top[0], NG).then_inc(logits_max, 1)
            dve.wait_ge(logits_max, 1)
            first_max(r_hot[0], r_dif[0], r_top[1], NG)
            dve.wait_ge(logits_exp, 1)
            link(dve.tensor_reduce(r_top[2], r_exp[0], AX, ALU.add))
            link(dve.reciprocal(r_top[2], r_top[2]))
            for t in range(NT):
                ins = dve.tensor_tensor(r_prod[:, t], lg[:, t, NG:].rearrange("p (g e) -> p g e", g=NG),
                                        r_hot[0][:, t, :].unsqueeze(2).to_broadcast([P, NG, EPG]), ALU.mult)
            link(ins)
            link(dve.tensor_reduce(r_sel, r_prod.rearrange("p t g e -> p t e g"), AX, ALU.add))
            minus_max(r_dif[1], r_sel, r_top[0], EPG).then_inc(logits_max, 1)
            dve.wait_ge(logits_exp, 2)
            for n in range(2):
                link(minus_max(r_dif[1], r_exp[1], r_top[3 + n], EPG))
                first_max(r_hot[1 + n], r_dif[1], r_top[0], EPG)
                if n == 0:
                    link(dve.scalar_tensor_tensor(r_exp[1], r_hot[1], -4.0, r_exp[1], ALU.mult, ALU.add))
            link(dve.tensor_tensor(r_top[0], r_top[3], r_top[4], ALU.add))
            link(dve.reciprocal(r_top[0], r_top[0]))
            link(dve.tensor_tensor(r_top[0], r_top[0], r_top[2], ALU.mult))
            for n in range(2):
                link(dve.tensor_tensor(r_top[3 + n], r_top[3 + n], r_top[0], ALU.mult))
                link(dve.tensor_tensor((r_sel, r_dif[1])[n], r_hot[1 + n], spread(r_top[3 + n], NT, EPG), ALU.mult))
            link(dve.tensor_tensor(r_sel, r_sel, r_dif[1], ALU.add))
            link(dve.tensor_tensor(r_hot[1], r_hot[1], r_hot[2], ALU.add))
            for dst, src in [(gate, r_sel), (mask, r_hot[1])]:
                for t in range(NT):
                    ins = dve.tensor_tensor(dst[:, t].rearrange("p (g e) -> p g e", g=NG),
                                            r_hot[0][:, t, :].unsqueeze(2).to_broadcast([P, NG, EPG]),
                                            src[:, t, :].unsqueeze(1).to_broadcast([P, NG, EPG]), ALU.mult)
            ins.then_inc(mask_ready, 1)
            dve.wait_ge(mask_ready, 1)
            g = G["pos"]
            full(dve, g)
            link(dve.scalar_tensor_tensor(posm, bank[g % 8][:, 0:2 * NE].rearrange("p (t e) -> p t e", t=NT), 1.0, mask,
                                          ALU.add, ALU.mult))
            link(dve.tensor_scalar(posm, posm, -1.0, None, ALU.add))
            dve.tensor_reduce(st[:, 25:26], bank[g % 8][:, 2 * NE:3 * NE], AX, ALU.max).then_inc(bank_moved[g % 8], 1)
            moved(dve, g)
            dve.tensor_scalar(flag[:, :], st[:, 25:26], CAP + 0.5, None, ALU.is_gt).then_inc(flag_ready, 1)

            iota = cs[:, C_IOTA:C_IOTA + CAP].unsqueeze(1).to_broadcast([P, 2, CAP])

            def of_pair(ap, t, i):
                return ap[:, t, bass.ds(2 * i, 2)].unsqueeze(2).to_broadcast([P, 2, CAP])

            def select(n, i):
                for t in range(NT):
                    ins = dve.tensor_tensor(Sel[:, t], iota, of_pair(posm, t, i), ALU.is_equal)
                ins.then_inc(sel_ready, 1)

            def take(n):
                for q in range(2):
                    dve.wait_ge(xg_full, 1 + q + 2 * n)
                    dve.tensor_copy(XgT[:, 4 * q:4 * q + 4, :], blocks(bank[2 + q], 4)).then_inc(xg_ready, 1)

            def pair(n, i, last=False):
                dve.wait_ge(sel_ready, 1 + n)
                for t in range(NT):
                    ins = dve.tensor_tensor(SelG[:, t], Sel[:, t], of_pair(gate, t, i), ALU.mult)
                ins.then_inc(selg_ready, 1)
                if not last:
                    dve.wait_ge(selg_ready, 1 + n)
                    select(n + 1, i + 1)
                dve.wait_ge(h3_full, 1 + n)
                dve.wait_ge(silu_ready, 1 + n)
                dve.tensor_tensor(hid, silu, bank[1][:, :], ALU.mult).then_inc(hidden_ready, 1)
                if not last:
                    take(n + 1)
                dve.wait_ge(sgT_full, 1 + n)
                dve.tensor_copy(SgT.rearrange("p a b -> p (a b)"), bank[0][:, 0:NT * P]).then_inc(sgT_ready, 1)

            def one_round(base):
                select(base, 0)
                take(base)
                with dve.Fori(0, NP - 1) as i:
                    pair(base + i, i)
                pair(base + (NP - 1), NP - 1, last=True)

            one_round(0)
            over = dve.value_load(flag[0:1, 0:1], min_val=0, max_val=1)
            with dve.If(over):
                with dve.Fori(1, ROUNDS) as r:
                    dve.tensor_scalar(posm, posm, -float(CAP), None, ALU.add).then_inc(pos_step, 1)
                    dve.wait_ge(pos_step, r)
                    one_round(r * NP)

            for t in range(NT):
                for hf in range(2):
                    dve.wait_ge(moe_full, 2 * t + hf + 1)
                    x = h[:, t, 512 * hf:512 * hf + 512]
                    ins = dve.tensor_tensor(x, x, bank[4 + 2 * t + hf][:, :], ALU.add)
                ins.then_inc(h_ready, 1)
            dve.wait_ge(h_squares, 14)
            refined(st[:, 16:18], st[:, 0:2])
            dve.wait_ge(gpost_here, 5 * 16)
            for t in range(NT):
                dve.scalar_tensor_tensor(xn[:, t, :], h[:, t, :], st[:, 16 + t:17 + t], gpost[:, :],
                                         ALU.mult, ALU.mult).then_inc(out_ready, 1)


_INS = ["x", "norm_g", "ffn_w_up", "ffn_conv_w", "ffn_conv_b", "ffn_w_down", "mla_w_dq", "mla_q_norm_g", "mla_w_uq",
        "mla_w_dkv", "mla_kv_norm_g", "mla_w_ukv", "mla_w_o", "diff_w_qkv", "diff_lambda", "diff_subln_g", "diff_w_o",
        "g_mix_2", "w_in_2", "w_proj_a_2", "w_proj_b_2", "w_out_2", "g_ffn_2", "w_group_2", "b_group_2", "w_expert_2",
        "b_expert_2", "w1_2", "w3_2", "w2_2", "g_final_2"]


def kernel(**inputs):
    import concourse.bacc as _bacc
    from concourse.bass_utils import run_bass_kernel_spmd as _run

    nc = _bacc.Bacc("TRN2", target_bir_lowering=False, num_devices=1)
    arrays, aps = {}, {}
    for name in _INS:
        a = np.ascontiguousarray(inputs[name])
        arrays[f"in_{name}"] = a
        aps[name] = nc.dram_tensor(f"in_{name}", a.shape, mybir.dt.from_np(a.dtype), kind="ExternalInput").ap()
    arrays["constants"] = constants()
    cst = nc.dram_tensor("constants", (P, C_END), F32, kind="ExternalInput").ap()
    out = nc.dram_tensor("out", (1, S, D), F32, kind="ExternalOutput").ap()
    build(nc, aps, cst, out)
    r = _run(nc, [arrays], core_ids=[0])
    return r.results[0]["out"]
```
